# Optimizing a Trainium2 kernel written in Bass

```python
import math
import jax, jax.numpy as jnp
from jax import lax
import numpy as np

D_MODEL = 2048
BATCH = 1
SEQ = 256
DEPTH = 2

N_A_LAYERS = DEPTH // 2
N_B_LAYERS = DEPTH - N_A_LAYERS
HEAD_DIM = 128
N_HEADS = D_MODEL // HEAD_DIM
DILATED_GROUPS = ((128, 1), (512, 4), (2048, 16))
N_GROUPS = len(DILATED_GROUPS)
ATTN_BLOCK = 128
CONV_WIDTH = 31
D_FF = 4 * D_MODEL
PLE_DIM = 256
ROPE_THETA = 10000.0
LN_EPS = 1e-5
DEEPNORM_ALPHA = (2 * DEPTH) ** 0.25
DEEPNORM_BETA = (8 * DEPTH) ** -0.25

kernel_name = "yoco_conformer_dilated_hybrid"

def layer_norm(x, g, b):
    xf = x.astype(jnp.float32)
    mu = jnp.mean(xf, axis=-1, keepdims=True)
    var = jnp.mean(jnp.square(xf - mu), axis=-1, keepdims=True)
    y = (xf - mu) * lax.rsqrt(var + LN_EPS) * g.astype(jnp.float32) + b.astype(jnp.float32)
    return y.astype(x.dtype)

def rotary(x, positions):
    half = HEAD_DIM // 2
    inv_freq = ROPE_THETA ** (-jnp.arange(half, dtype=jnp.float32) * (2.0 / HEAD_DIM))
    ang = positions.astype(jnp.float32)[..., None] * inv_freq
    cos = jnp.cos(ang)[:, :, None, :]
    sin = jnp.sin(ang)[:, :, None, :]
    xf = x.astype(jnp.float32)
    x1, x2 = xf[..., :half], xf[..., half:]
    return jnp.concatenate([x1 * cos - x2 * sin, x2 * cos + x1 * sin], axis=-1).astype(x.dtype)

def conformer_conv(x, w_in, b_in, dw, dw_b, ln_g, ln_b, w_out):
    u = x @ w_in + b_in
    a, g = jnp.split(u, 2, axis=-1)
    u = a * jax.nn.sigmoid(g)
    u = lax.conv_general_dilated(
        u, dw.astype(u.dtype), window_strides=(1,), padding=[(CONV_WIDTH - 1, 0)],
        dimension_numbers=("NWC", "WIO", "NWC"), feature_group_count=D_MODEL) + dw_b
    u = jax.nn.silu(layer_norm(u, ln_g, ln_b))
    return u @ w_out

def to_strided_blocks(t, dil):
    b_, s_pad, h, hd = t.shape
    length = s_pad // dil
    t = t.reshape(b_, length, dil, h, hd).transpose(0, 2, 3, 1, 4)
    return t.reshape(b_, dil, h, length // ATTN_BLOCK, ATTN_BLOCK, hd)

def with_previous_block(t):
    prev = jnp.pad(t, ((0, 0), (0, 0), (0, 0), (1, 0), (0, 0), (0, 0)))[:, :, :, :-1]
    return jnp.concatenate([prev, t], axis=4)

def dilated_window_attention(q, k, v, window, dil):
    n_back = window // dil
    b_, s, h, hd = q.shape
    span = dil * ATTN_BLOCK
    s_pad = -(-s // span) * span
    pad = ((0, 0), (0, s_pad - s), (0, 0), (0, 0))
    qb = to_strided_blocks(jnp.pad(q, pad), dil)
    kk = with_previous_block(to_strided_blocks(jnp.pad(k, pad), dil))
    vv = with_previous_block(to_strided_blocks(jnp.pad(v, pad), dil))
    nb = qb.shape[3]
    sc = jnp.einsum("brhnqc,brhnkc->brhnqk", qb, kk,
                    preferred_element_type=jnp.float32) * (HEAD_DIM ** -0.5)
    qi = jnp.arange(ATTN_BLOCK)[:, None]
    kj = jnp.arange(2 * ATTN_BLOCK)[None, :]
    delta = qi + ATTN_BLOCK - kj
    key_sub = jnp.arange(nb)[:, None, None] * ATTN_BLOCK + kj - ATTN_BLOCK
    valid = (delta >= 0) & (delta <= n_back) & (key_sub >= 0)
    sc = jnp.where(valid, sc, -jnp.inf)
    m = jnp.max(sc, axis=-1, keepdims=True)
    pexp = jnp.exp(sc - m)
    l = jnp.sum(pexp, axis=-1, keepdims=True)
    o = jnp.einsum("brhnqk,brhnkc->brhnqc", pexp, vv.astype(jnp.float32)) / l
    lse = (m + jnp.log(l))[..., 0]
    o = o.transpose(0, 3, 4, 1, 2, 5).reshape(b_, s_pad, h, hd)[:, :s]
    lse = lse.transpose(0, 3, 4, 1, 2).reshape(b_, s_pad, h)[:, :s]
    return o, lse

def shared_kv(x, g, b, w_kv, positions):
    b_, s, _ = x.shape
    kv = (layer_norm(x, g, b) @ w_kv).reshape(b_, s, 2, N_HEADS, HEAD_DIM)
    return rotary(kv[:, :, 0], positions), kv[:, :, 1]

def dilated_mixer(x, w_q, k, v, w_o, positions):
    b_, s, _ = x.shape
    q = (x @ w_q).reshape(b_, s, N_GROUPS, N_HEADS, HEAD_DIM)
    outs, lses = [], []
    for g, (window, dil) in enumerate(DILATED_GROUPS):
        o, lse = dilated_window_attention(rotary(q[:, :, g], positions), k, v, window, dil)
        outs.append(o)
        lses.append(lse)
    wts = jax.nn.softmax(jnp.stack(lses), axis=0)
    o = jnp.sum(wts[..., None] * jnp.stack(outs), axis=0)
    return o.reshape(b_, s, D_MODEL).astype(x.dtype) @ w_o

def sq_relu_mlp(x, w_up, w_down):
    return jnp.square(jax.nn.relu(x @ w_up)) @ w_down

def per_layer_embedding(x, p_i, w_proj, w_gate):
    return (p_i @ w_proj) * jax.nn.sigmoid(x @ w_gate)

def setup_inputs(seed: int = 0) -> dict:
    key = jax.random.key(seed)
    ks = jax.random.split(key, 24)
    f32 = jnp.float32
    D = D_MODEL

    def w(k, shape, fan_in, scale=1.0):
        return jax.random.normal(k, shape, f32) * (fan_in ** -0.5) * scale

    def gain(k, shape):
        return 1.0 + 0.02 * jax.random.normal(k, shape, f32)

    def bias(k, shape):
        return 0.02 * jax.random.normal(k, shape, f32)

    x = jax.random.normal(ks[0], (BATCH, SEQ, D), f32)
    p = jax.random.normal(ks[1], (DEPTH, BATCH, SEQ, PLE_DIM), f32)
    offsets = jax.random.randint(ks[2], (BATCH, 1), 0, 1024, dtype=jnp.int32)
    positions = (jnp.arange(SEQ, dtype=jnp.int32)[None, :] + offsets).astype(jnp.int32)

    w_k = w(ks[10], (D, D), D)
    w_v = w(ks[11], (D, D), D, DEEPNORM_BETA)
    w_kv = jnp.concatenate([w_k, w_v], axis=-1)

    return {
        "x": x,
        "p": p,
        "positions": positions,
        "conv_w_in": w(ks[3], (N_A_LAYERS, D, 2 * D), D),
        "conv_b_in": bias(ks[4], (N_A_LAYERS, 2 * D)),
        "conv_dw": w(ks[5], (N_A_LAYERS, CONV_WIDTH, 1, D), CONV_WIDTH),
        "conv_dw_b": bias(ks[6], (N_A_LAYERS, D)),
        "conv_ln_g": gain(ks[7], (N_A_LAYERS, D)),
        "conv_ln_b": bias(ks[8], (N_A_LAYERS, D)),
        "conv_w_out": w(ks[9], (N_A_LAYERS, D, D), D, DEEPNORM_BETA),
        "kv_ln_g": gain(ks[12], (D,)),
        "kv_ln_b": bias(ks[13], (D,)),
        "w_kv": w_kv,
        "attn_w_q": w(ks[14], (N_B_LAYERS, D, N_GROUPS * D), D),
        "attn_w_o": w(ks[15], (N_B_LAYERS, D, D), D, DEEPNORM_BETA),
        "ln1_g": gain(ks[16], (DEPTH, D)),
        "ln1_b": bias(ks[17], (DEPTH, D)),
        "mlp_up": w(ks[18], (DEPTH, D, D_FF), D),
        "mlp_down": w(ks[19], (DEPTH, D_FF, D), D_FF, DEEPNORM_BETA),
        "ln2_g": gain(ks[20], (DEPTH, D)),
        "ln2_b": bias(ks[21], (DEPTH, D)),
        "ple_proj": w(ks[22], (DEPTH, PLE_DIM, D), PLE_DIM),
        "ple_gate": w(ks[23], (DEPTH, D, D), D),
    }

def reference(x, p, positions, conv_w_in, conv_b_in, conv_dw, conv_dw_b, conv_ln_g, conv_ln_b,
              conv_w_out, kv_ln_g, kv_ln_b, w_kv, attn_w_q, attn_w_o, ln1_g, ln1_b, mlp_up, mlp_down,
              ln2_g, ln2_b, ple_proj, ple_gate):
    k = v = None
    for i in range(DEPTH):
        if i < N_A_LAYERS:
            mix = conformer_conv(x, conv_w_in[i], conv_b_in[i], conv_dw[i], conv_dw_b[i],
                                 conv_ln_g[i], conv_ln_b[i], conv_w_out[i])
        else:
            j = i - N_A_LAYERS
            mix = dilated_mixer(x, attn_w_q[j], k, v, attn_w_o[j], positions)
        x = layer_norm(DEEPNORM_ALPHA * x + mix, ln1_g[i], ln1_b[i])
        x = layer_norm(DEEPNORM_ALPHA * x + sq_relu_mlp(x, mlp_up[i], mlp_down[i]), ln2_g[i], ln2_b[i])
        x = x + per_layer_embedding(x, p[i], ple_proj[i], ple_gate[i])
        if i == N_A_LAYERS - 1:
            k, v = shared_kv(x, kv_ln_g, kv_ln_b, w_kv, positions)
    return x


_drawn_inputs = setup_inputs


def setup_inputs(seed=0):
    import zlib

    import numpy as np

    out = dict(_drawn_inputs(seed))
    spreads = {}
    factors = {'conv_b_in': 8.0,
     'conv_dw_b': 7.144,
     'conv_ln_g': 8.0,
     'conv_ln_b': 8.0,
     'kv_ln_g': 8.0,
     'kv_ln_b': 8.0}
    for name, (base, spread) in spreads.items():
        noise = np.random.default_rng([zlib.crc32(name.encode()), seed]).standard_normal(out[name].shape)
        drawn = base * np.exp(spread * noise) if base else spread * noise
        out[name] = __import__('jax').numpy.asarray(drawn.astype(out[name].dtype))
    for name, factor in factors.items():
        out[name] = (out[name] * factor).astype(out[name].dtype)
    return out
```

```python
from contextlib import ExitStack

import numpy as np

import concourse.bass as bass
from concourse import mybir

F32 = mybir.dt.float32
F32R = mybir.dt.float32r
BF16 = mybir.dt.bfloat16
I32 = mybir.dt.int32
ALU = mybir.AluOpType
ACT = mybir.ActivationFunctionType

P = 128
D = 2048
T = 256
TT = T // P
KT = D // P
F = 4 * D
COLS = 512
CHUNKS = D // COLS
PIECES = 8
KP = KT // PIECES
RAW = 4
TAPS = 31
PAD = TAPS - 1
HD = 128
HALF = HD // 2
HEADS = D // HD
HPU = COLS // HD
WINDOWS = ((128, 1), (512, 4), (2048, 16))
G = len(WINDOWS)
PLE = 256
DEPTH = 2
ALPHA = float((2 * DEPTH) ** 0.25)
EPS = 1e-5
SCALE = float(HD) ** -0.5
MASKED = -3.0e38
KEYS = (P, T)
PARAMS = TAPS + 3

UNITS = dict(conv=8, conv_out=4, mlp0=32, proj0=0, gate0=4, kv=8, q=12, attn_out=4, mlp1=32, proj1=0, gate1=4)
UNIT, QUARTER, GROUP, HIGH, ROWS = {}, {}, {}, {}, {}
_u = _q = 0
for _s, _n in UNITS.items():
    UNIT[_s], QUARTER[_s] = _u, _q
    _u += _n
    _q += 2 * _n if _n else 1
NORMS = ("conv_ln", "ln1_0", "ln2_0", "kv_ln", "ln1_1", "ln2_1")
_g = _h = _r = 0
for _s, _n in (("x", 4), ("conv_ln", 4), ("ln1_0", 4), ("p0", 1), ("mlp0", 16), ("ln2_0", 4), ("gate0", 4),
               ("kv_ln", 4), ("k", 4), ("o", 4), ("ln1_1", 4), ("p1", 1), ("mlp1", 16), ("ln2_1", 4)):
    GROUP[_s], HIGH[_s], ROWS[_s] = _g, _h, _r
    _g += _n
    _h += _n if _s != "k" else 0
    _r += _n if _s in NORMS else 0

SCORES = {4 + 4 * n: n for n in range(HPU)}
TURN_P = {6 + 4 * n: n for n in range(HPU)}
PV = {7 + 4 * n: n for n in range(HPU)}
TURN_Q = {2: (2, 0), 3: (2, 1), 17: (0, 0), 19: (0, 1), 21: (1, 0), 23: (1, 1)}
ROTATE = {0: 2, 8: 0, 20: 1}
BLOCKS = HEADS // HPU


class Count:

    def __init__(self, engine, sem):
        self.engine, self.sem, self.n, self.off = engine, sem, 0, 0

    def mark(self, instruction):
        instruction.then_inc(self.sem, 1)
        self.n += 1
        return self.n

    def wait(self, value):
        self.engine.wait_ge(self.sem, self.off + value)

    def link(self, instruction):
        self.wait(self.mark(instruction))

    def enter(self, i, by):
        self.off, self.by, self.at = i * by, by, self.n

    def leave(self, rounds):
        assert self.n - self.at == self.by, (self.n - self.at, self.by)
        self.off, self.n = 0, self.at + self.by * rounds


def trunk(nc, A, out):
    with ExitStack() as ctx:
        place = {"at": -(-nc.sbuf_base // 32) * 32}

        def region(nbytes):
            here = place["at"]
            place["at"] = here + -(-nbytes // 8) * 8
            return here

        def at(name, shape, dt, offset):
            return nc.alloc_sbuf_tensor_at(name, shape, dt, offset=offset, align_bytes=8)

        def small(name, shape, dt=F32):
            return at(name, shape, dt, region(int(np.prod(shape[1:])) * 4))

        PIECE = KP * COLS * 4
        SPLIT = KT * T * 4
        raw = at("raw", [P, RAW, KP, COLS], F32, region(RAW * PIECE))
        w_hi = at("w_hi", [P, PIECES, KP, COLS], F32R, region(PIECES * PIECE))
        w_lo = at("w_lo", [P, PIECES, KP, COLS], F32R, region(PIECES * PIECE))

        r_a = region(2 * SPLIT)
        a_hi = at("a_hi", [P, KT, T], F32R, r_a)
        a_lo = at("a_lo", [P, KT, T], F32R, r_a + SPLIT)
        o_tok = at("o_tok", [P, TT, D], F32, r_a)
        q_t = at("q_t", [P, G, HPU, T], F32, r_a + SPLIT)
        q_rot = at("q_rot", [P, TT, COLS], F32, r_a + SPLIT + G * HPU * T * 4)

        r_b = region(2 * SPLIT)
        b_hi = at("b_hi", [P, KT, T], F32R, r_b)
        b_lo = at("b_lo", [P, KT, T], F32R, r_b + SPLIT)
        params = at("params", [P, KT, PARAMS], F32, r_b)
        dw_rows = at("dw_rows", [TAPS, D], F32, r_b + 4096)
        bias_rows = at("bias_rows", [3 * KT, P], F32, r_b + 4096 + D * 4)
        mask_f = at("mask_f", [P, G * sum(KEYS)], F32, r_b + SPLIT)

        r_g = region(2 * D * 4)
        gain = at("gain", [P, D], F32, r_g)
        shift = at("shift", [P, D], F32, r_g + D * 4)
        k_t = at("k_t", [P, HEADS, T], F32, r_g)

        r_v = region(TT * D * 4)
        v_tok = at("v_tok", [P, TT, D], F32, r_v)
        inv_freq = at("inv_freq", [P, HALF], F32, r_v)
        angle = at("angle", [P, TT, HALF], F32, r_v + 1024)
        turns = at("turns", [P, TT, HALF], F32, r_v + 2048)
        for_cos = at("for_cos", [P, TT, HALF], F32, r_v + 3072)
        for_sin = at("for_sin", [P, TT, HALF], F32, r_v + 4096)

        pos_i = at("pos_i", [P, TT], I32, r_v + 5120)
        pos_f = at("pos_f", [P, TT], F32, r_v + 5152)

        x_tok = small("x_tok", [P, TT, D])

        r_s = region(2 * G * sum(KEYS) * 4)
        s_tok = at("s_tok", [P, TT, COLS], F32, r_s)
        p_hi = at("p_hi", [P, PLE // P, T], F32R, r_s + 4096)
        p_lo = at("p_lo", [P, PLE // P, T], F32R, r_s + 6144)
        silu = at("silu", [P, 2, 4 * T], F32, r_s)
        u_pad = at("u_pad", [P, 2, PAD + T], F32, r_s)
        sig = at("sig", [P, 2, T], F32, r_s + 2304)
        c_copy = at("c_copy", [P, 2, T], F32, r_s + 4352)
        taps = at("taps", [P, 2, PARAMS], F32, r_s + 6400)
        soft = at("soft", [P, 2, G * sum(KEYS)], F32, r_s)

        mask = at("mask", [P, G * sum(KEYS)], BF16, region(G * sum(KEYS) * 2))
        ident = small("ident", [P, P])
        cos_t = small("cos_t", [P, TT, HALF])
        sin_t = small("sin_t", [P, TT, HALF])
        nsin_t = small("nsin_t", [P, TT, HALF])
        r_rot = region(COLS * 4)
        rot_tmp = at("rot_tmp", [P, COLS], F32, r_rot)
        p_tok = at("p_tok", [P, TT, PLE], F32, r_rot)
        stats = small("stats", [P, TT, 8, 6])
        mean_var = small("mean_var", [P, TT, 2])
        std = small("std", [P, TT])
        rstd = small("rstd", [P, TT])
        row_max = small("row_max", [P, 2, TT])
        neg_max = small("neg_max", [P, 2, TT])
        row_sum = small("row_sum", [P, 2, TT])
        row_inv = small("row_inv", [P, 2, TT])
        eps = small("eps", [P, 1])
        assert place["at"] <= nc.sbuf_top, (place["at"], nc.sbuf_top)

        bank = ctx.enter_context(nc.psum_tensor("bank", [P, 8, COLS], F32))

        def pair(n):
            return bank[:, 2 * (n % 2):2 * (n % 2) + 2, :]

        def group_out(g):
            b = 4 + 2 * (g % 2)
            return bank[:, b:b + 2, :].rearrange("p b (k t) -> p (b k) t", t=T)

        S1, S0, TURN = 4, 6, 7

        def sem(name):
            return ctx.enter_context(nc.semaphore(name))

        landed = [sem(f"landed{i}") for i in range(RAW)]
        hi_done = sem("hi_done")
        lo_done = sem("lo_done")
        used = sem("used")
        pair_free = sem("pair_free")
        x_landed = [sem(f"x_landed{i}") for i in range(CHUNKS)]
        const_landed = sem("const_landed")
        rows_landed = sem("rows_landed")
        p_landed = sem("p_landed")
        gain_landed = sem("gain_landed")
        params_turned = sem("params_turned")
        params_done = sem("params_done")
        angles_done = sem("angles_done")
        sines_done = sem("sines_done")
        mask_done = sem("mask_done")
        rows_ready = sem("rows_ready")
        group_done = sem("group_done")
        group_hi = sem("group_hi")
        group_free = sem("group_free")
        sig_done = sem("sig_done")
        conv_done = sem("conv_done")
        conv_copied = sem("conv_copied")
        conv_turned = sem("conv_turned")
        conv_stored = sem("conv_stored")
        relu_done = sem("relu_done")
        var_done = sem("var_done")
        std_done = sem("std_done")
        scaled = sem("scaled")
        proj_stored = sem("proj_stored")
        gate_done = sem("gate_done")
        x_new = sem("x_new")
        q_rotated = sem("q_rotated")
        q_turned = sem("q_turned")
        q_copied = sem("q_copied")
        scores_done = sem("scores_done")
        soft_ready = sem("soft_ready")
        exp_done = sem("exp_done")
        prob_done = sem("prob_done")
        prob_turned = sem("prob_turned")
        prob_copied = sem("prob_copied")
        o_done = sem("o_done")
        o_stored = sem("o_stored")
        act_step = sem("act_step")
        dve_step = sem("dve_step")
        stored = sem("stored")

        def rows(w):
            return w.rearrange("(kt p) n -> p kt n", p=P)

        w_in, w_conv, w_kv, w_q, w_o = (rows(w) for w in (A["conv_w_in"][0], A["conv_w_out"][0], A["w_kv"], A["attn_w_q"][0], A["attn_w_o"][0]))
        w_up = [rows(A["mlp_up"][n]) for n in range(DEPTH)]
        w_down = [rows(A["mlp_down"][n]) for n in range(DEPTH)]
        w_proj = [rows(A["ple_proj"][n]) for n in range(DEPTH)]
        w_gate = [rows(A["ple_gate"][n]) for n in range(DEPTH)]
        x_rows = A["x"][0].rearrange("(t p) n -> p t n", p=P)
        out_rows = out[0].rearrange("(t p) n -> p t n", p=P)
        norm_rows = [(A["conv_ln_g"][0:1, :], A["conv_ln_b"][0:1, :]),
                     (A["ln1_g"][0:1, :], A["ln1_b"][0:1, :]), (A["ln2_g"][0:1, :], A["ln2_b"][0:1, :]),
                     tuple(A[n].rearrange("(a n) -> a n", a=1) for n in ("kv_ln_g", "kv_ln_b")),
                     (A["ln1_g"][1:2, :], A["ln1_b"][1:2, :]), (A["ln2_g"][1:2, :], A["ln2_b"][1:2, :])]

        def chunk(c):
            return slice(c * COLS, (c + 1) * COLS)

        def parity(stage):
            return 4 * (QUARTER[stage] % 2)

        def seen(t, g=0):
            return G * sum(KEYS[:t]) + g * KEYS[t]

        def prob_t(b):
            return soft[:, b, seen(1, 1):seen(1, 1) + sum(KEYS)]

        block = ctx.enter_context(nc.Block())

        @block.sync
        def _(sp):
            def piece(source, q, e, first=False):
                dst = raw[:, e % RAW, :, :]
                if source.shape[1] != KP:
                    dst = dst.rearrange("p k (h n) -> p (k h) n", h=2)
                if not first:
                    sp.wait_ge(lo_done, 4 * q + e - (RAW - 1))
                sp.dma_start(dst, source).then_inc(landed[e % RAW], 16)

            def unit(w, q, col, row=0):
                for e in range(PIECES):
                    piece(w[:, bass.ds(row + KP * e, KP), bass.ds(col, COLS)], q, e)

            def units(w, stage, n):
                with sp.Fori(0, n) as i:
                    unit(w, QUARTER[stage] + 2 * i, i * COLS)

            def mlp(layer):
                q0 = QUARTER[f"mlp{layer}"]
                with sp.Fori(0, F // D) as s:
                    for c in range(CHUNKS):
                        unit(w_up[layer], q0 + 2 * c + 16 * s, s * D + c * COLS)
                    for c in range(CHUNKS):
                        unit(w_down[layer], q0 + 8 + 2 * c + 16 * s, c * COLS, row=s * KT)

            def ple(layer):
                for c in range(CHUNKS):
                    piece(w_proj[layer][:, :, chunk(c)], QUARTER[f"proj{layer}"], c)
                units(w_gate[layer], f"gate{layer}", CHUNKS)

            def conv_piece(i, e, first=False):
                rows_ = slice(2 * KP * (e // 2), 2 * KP * (e // 2 + 1))
                piece(w_in[:, rows_, bass.ds(i * (COLS // 2) + e % 2 * D, COLS // 2)], 2 * i, e, first)

            for e in range(PIECES):
                conv_piece(0, e, first=e < RAW)
            with sp.Fori(1, UNITS["conv"]) as i:
                for e in range(PIECES):
                    conv_piece(i, e)
            units(w_conv, "conv_out", 4)
            mlp(0)
            ple(0)
            units(w_kv, "kv", 8)
            with sp.Fori(0, BLOCKS) as i:
                for g in range(G):
                    unit(w_q, QUARTER["q"] + 2 * g + 2 * G * i, g * D + i * COLS)
            units(w_o, "attn_out", 4)
            mlp(1)
            ple(1)
            sp.wait_ge(stored, 16 * CHUNKS)

        @block.gpsimd
        def _(pool):
            pool.dma_start(ident[:, :], A["consts"][:, 0:P]).then_inc(const_landed, 16)
            pool.dma_start(dw_rows[:, :], A["conv_dw"][0].rearrange("w a n -> w (a n)")).then_inc(rows_landed, 16)
            pool.dma_start(bias_rows[0:2 * KT, :], A["conv_b_in"][0].rearrange("(r n) -> r n", n=P)).then_inc(rows_landed, 16)
            pool.dma_start(bias_rows[2 * KT:3 * KT, :], A["conv_dw_b"][0].rearrange("(r n) -> r n", n=P)).then_inc(rows_landed, 16)
            pool.dma_start(inv_freq[:, :], A["consts"][:, P:P + HALF]).then_inc(const_landed, 16)
            pool.dma_start(mask_f[:, :], A["consts"][:, P + HALF:]).then_inc(const_landed, 16)
            with nc.allow_non_contiguous_dma(reason="256 numbers"):
                pool.dma_start(pos_i[:, :], A["positions"].rearrange("b (t p) -> p (b t)", p=P)).then_inc(const_landed, 16)

            def load_gains(k):
                for dst, row in zip((gain, shift), norm_rows[k]):
                    pool.dma_start(dst[:, :], row.partition_broadcast(P)).then_inc(gain_landed, 16)

            def load_p(layer):
                pool.dma_start(p_tok[:, :, :], A["p"][layer, 0].rearrange("(t p) n -> p t n", p=P)).then_inc(p_landed, 16)

            def split_lo(q, e):
                pool.wait_ge(hi_done, 4 * q + e + 1)
                nc.gpsimd.tensor_tensor(w_lo[:, e, :, :], raw[:, e % RAW, :, :], w_hi[:, e, :, :],
                                        ALU.subtract).then_inc(lo_done, 1)

            load_gains(0)
            load_p(0)
            with pool.Fori(0, UNITS["conv"] + 1) as i:
                for e in range(PIECES):
                    split_lo(2 * i, e)
            for k in range(1, len(NORMS)):
                if k == NORMS.index("ln1_1"):
                    pool.wait_ge(soft_ready, HEADS)
                    load_p(1)
                else:
                    pool.wait_ge(rows_ready, ROWS[NORMS[k - 1]] + CHUNKS)
                load_gains(k)

        @block.scalar
        def _(act):
            step = Count(act, act_step)

            def split_hi(q, e, turned, first=False):
                slot = (e + turned) % PIECES
                act.wait_ge(landed[e % RAW], 16 * (q + e // RAW) + 16)
                if not first:
                    act.wait_ge(used, 4 * q + e - (PIECES - 1))
                nc.scalar.activation(w_hi[:, slot, :, :], raw[:, e % RAW, :, :], ACT.Copy).then_inc(hi_done, 1)

            def splits(q, turned, pieces):
                for e in pieces:
                    split_hi(q + 2, e, turned)

            def group_to_hi(g, dst, kt, off=0, blocks=4):
                act.wait_ge(group_done, off + g + 1)
                nc.scalar.activation(dst[:, kt:kt + blocks, :], group_out(g)[:, 0:blocks, :], ACT.Copy).then_inc(group_hi, 1)

            def norm(k):
                g0 = GROUP[NORMS[k]]
                act.wait_ge(var_done, k + 1)
                nc.scalar.activation(std[:, :], mean_var[:, :, 1], ACT.Sqrt, bias=eps[:, 0:1]).then_inc(std_done, 1)
                yield
                for c in range(CHUNKS):
                    if k == 0:
                        act.wait_ge(group_done, g0 + c + 1)
                        if c >= 2:
                            act.wait_ge(group_free, g0 + c - 1)
                        buf = silu[:, c % 2, :].rearrange("p (k t) -> p k t", t=T)
                        step.link(nc.scalar.activation(buf, group_out(g0 + c), ACT.Silu))
                        nc.scalar.activation(a_hi[:, 4 * c:4 * c + 4, :], buf, ACT.Copy).then_inc(group_hi, 1)
                    else:
                        group_to_hi(g0 + c, a_hi, 4 * c)
                    if NORMS[k].startswith("ln1"):
                        nc.scalar.activation(x_tok[:, :, chunk(c)], x_tok[:, :, chunk(c)], ACT.Copy, scale=ALPHA).then_inc(scaled, 1)
                    yield

            def run(steps):
                for _ in steps:
                    pass

            for c in range(CHUNKS):
                act.dma_start(x_tok[:, :, chunk(c)], x_rows[:, :, chunk(c)]).then_inc(x_landed[c], 16)
            for c in range(CHUNKS):
                group_to_hi(GROUP["x"] + c, a_hi, 4 * c)
                split_hi(0, 2 * c, 0, first=True)
                split_hi(0, 2 * c + 1, 0, first=True)
            act.wait_ge(const_landed, 64)
            nc.scalar.activation(mask[:, :], mask_f[:, :], ACT.Copy).then_inc(mask_done, 1)
            act.wait_ge(angles_done, 1)
            nc.scalar.activation(cos_t[:, :, :], for_cos[:, :, :], ACT.Sin).then_inc(sines_done, 1)
            nc.scalar.activation(sin_t[:, :, :], for_sin[:, :, :], ACT.Sin).then_inc(sines_done, 1)

            def conv_store(j, half):
                act.wait_ge(conv_turned, j + 1)
                nc.scalar.activation(v_tok[:, :, bass.ds(j * T, T)], bank[:, 6 + half, :].rearrange("p (t n) -> p t n", t=TT),
                                     ACT.Copy).then_inc(conv_stored, 1)

            def conv_copy(j, half, first=False):
                act.wait_ge(conv_done, 2 * j + 2)
                if not first:
                    act.wait_ge(conv_turned, j)
                nc.scalar.activation(c_copy[:, :, :], bank[:, 4 + half, :].rearrange("p (k t) -> p k t", t=T),
                                     ACT.Copy).then_inc(conv_copied, 1)

            def conv_unit(j, q, half, first=False, store=True):
                splits(q, 0, range(0, 4))
                if store:
                    conv_store(j - 2, half)
                splits(q, 0, range(4, 7))
                act.wait_ge(used, 8 * j + 8)
                if not first:
                    act.wait_ge(pair_free, j + 2)
                for k in range(2):
                    nc.scalar.activation(sig[:, k, :], pair(half)[:, k, T:2 * T], ACT.Sigmoid,
                                         bias=params[:, bass.ds(2 * j + k, 1), PARAMS - 1]).then_inc(sig_done, 1)
                splits(q, 0, range(7, 8))

            act.wait_ge(params_done, 1)
            conv_unit(0, 0, 0, first=True, store=False)
            conv_unit(1, 2, 1, store=False)
            conv_copy(0, 0, first=True)
            with act.Fori(1, UNITS["conv"] // 2) as i:
                for k in range(2):
                    conv_unit(2 * i + k, 4 * i + 2 * k, k)
                    conv_copy(2 * i + k - 1, 1 - k)
            last = UNITS["conv"] - 1
            conv_store(last - 1, 0)
            conv_copy(last, 1)
            conv_store(last, 1)
            run(norm(0))

            def plain_units(stage):
                with act.Fori(0, UNITS[stage]) as i:
                    splits(QUARTER[stage] + 2 * i, parity(stage), range(PIECES))

            def mlp(layer):
                stage = f"mlp{layer}"
                run(norm(NORMS.index(f"ln1_{layer}")))
                group_to_hi(GROUP[f"p{layer}"], p_hi, 0, blocks=PLE // P)
                with act.Fori(0, F // D) as s:
                    for c in range(2 * CHUNKS):
                        q = QUARTER[stage] + 2 * c + 16 * s
                        splits(q, parity(stage), range(0, 2))
                        if 1 <= c <= CHUNKS:
                            group_to_hi(GROUP[stage] + c - 1, b_hi, 4 * (c - 1), off=4 * s)
                        splits(q, parity(stage), range(2, 7))
                        if c < CHUNKS:
                            act.wait_ge(used, 4 * q + 8)
                            for t in range(TT):
                                nc.scalar.activation(s_tok[:, t, :], pair(UNIT[stage] + c)[:, t, :], ACT.Relu).then_inc(relu_done, 1)
                        splits(q, parity(stage), range(7, 8))

            def ple(layer):
                proj, gate = f"proj{layer}", f"gate{layer}"
                steps = norm(NORMS.index(f"ln2_{layer}"))
                for c in range(CHUNKS + 1):
                    next(steps)
                    if c < CHUNKS:
                        act.wait_ge(used, 4 * QUARTER[proj] + c + 1)
                        nc.scalar.activation(v_tok[:, :, chunk(c)], pair(c), ACT.Copy).then_inc(proj_stored, 1)
                for e in range(4):
                    split_hi(QUARTER[proj] + 2, e, parity(proj))
                for c in range(CHUNKS):
                    q = QUARTER[gate] + 2 * c
                    more = range(PIECES) if layer < DEPTH - 1 or c < CHUNKS - 1 else ()
                    splits(q, parity(gate), more[0:2])
                    if c and layer == 0:
                        group_to_hi(GROUP[gate] + c - 1, b_hi, 4 * (c - 1))
                    splits(q, parity(gate), more[2:7])
                    act.wait_ge(used, 4 * q + 8)
                    if c and layer == 1:
                        act.wait_ge(stored, 16 * c)
                    if c and layer == 0:
                        step.wait(step.n)
                    for t in range(TT):
                        nc.scalar.activation(s_tok[:, t, :], pair(UNIT[gate] + c)[:, t, :], ACT.Sigmoid).then_inc(gate_done, 1)
                    act.wait_ge(x_new, CHUNKS * layer + c + 1)
                    if layer == 0:
                        step.mark(nc.scalar.activation(x_tok[:, :, chunk(c)], s_tok[:, :, :], ACT.Copy))
                    else:
                        act.dma_start(out_rows[:, :, chunk(c)], s_tok[:, :, :]).then_inc(stored, 16)
                    splits(q, parity(gate), more[7:8])
                if layer == 0:
                    step.wait(step.n)
                    group_to_hi(GROUP[gate] + CHUNKS - 1, b_hi, 4 * (CHUNKS - 1))

            plain_units("conv_out")
            mlp(0)
            ple(0)
            run(norm(NORMS.index("kv_ln")))
            plain_units("kv")

            def exps(h):
                act.wait_ge(soft_ready, h + 1)
                for t in range(TT):
                    s = soft[:, h % 2, seen(t):seen(t, G)]
                    nc.scalar.activation(s, s, ACT.Exp, bias=neg_max[:, h % 2, t:t + 1],
                                         accum_out=row_sum[:, h % 2, t:t + 1]).then_inc(exp_done, 1)

            def copy_probs(h):
                act.wait_ge(prob_turned, h + 1)
                nc.scalar.activation(prob_t(h % 2), bank[:, TURN, 0:sum(KEYS)], ACT.Copy).then_inc(prob_copied, 1)

            def store_o(h):
                act.wait_ge(o_done, h + 1)
                for t in range(TT):
                    nc.scalar.activation(o_tok[:, t, h * HD:(h + 1) * HD], bank[:, S0, t * HD:(t + 1) * HD], ACT.Copy,
                                         scale=row_inv[:, h % 2, t:t + 1]).then_inc(o_stored, 1)

            for i in range(BLOCKS):
                for gap in range(G * PIECES):
                    h = HPU * (i - 1)
                    if i and gap in SCORES:
                        exps(h + SCORES[gap])
                    if i and gap in TURN_P:
                        copy_probs(h + TURN_P[gap])
                    if i and gap in PV:
                        store_o(h + PV[gap])
                    q = QUARTER["q"] + 2 * (G * i + gap // PIECES)
                    split_hi(q + 2, gap % PIECES, parity("q"))
            for h in range(HEADS - HPU, HEADS):
                exps(h)
                copy_probs(h)
                store_o(h)
            for c in range(CHUNKS):
                group_to_hi(GROUP["o"] + c, b_hi, 4 * c)
            plain_units("attn_out")
            mlp(1)
            ple(1)

        @block.vector
        def _(dve):
            step = Count(dve, dve_step)
            link, mark = step.link, step.mark

            def split_lo(q, e, turned):
                slot = (e + turned) % PIECES
                dve.wait_ge(hi_done, 4 * q + e + 1)
                nc.vector.tensor_tensor(w_lo[:, slot, :, :], raw[:, e % RAW, :, :], w_hi[:, slot, :, :],
                                        ALU.subtract).then_inc(lo_done, 1)

            def splits(q, turned, pieces):
                for e in pieces:
                    split_lo(q + 2, e, turned)

            def group_to_lo(stage, c, hi, lo, kt, off=0, blocks=4, source=None):
                dve.wait_ge(group_hi, off + HIGH[stage] + c + 1)
                src = group_out(GROUP[stage] + c)[:, 0:blocks, :] if source is None else source
                nc.vector.tensor_tensor(lo[:, kt:kt + blocks, :], src, hi[:, kt:kt + blocks, :],
                                        ALU.subtract).then_inc(group_free, 1)

            def norm(k, parts, src, dst):
                name = NORMS[k]
                step.wait(step.n)
                nc.vector.bn_aggr(mean_var[:, 0, :], stats[:, 0, 0:parts, :])
                nc.vector.bn_aggr(mean_var[:, 1, :], stats[:, 1, 0:parts, :]).then_inc(var_done, 1)
                dve.wait_ge(std_done, k + 1)
                link(nc.vector.reciprocal(rstd[:, :], std[:, :]))
                dve.wait_ge(gain_landed, 32 * (k + 1))
                for c in range(CHUNKS + 1):
                    if c < CHUNKS:
                        centred = [mark(nc.vector.scalar_tensor_tensor(
                            dst[:, t, chunk(c)], src[:, t, chunk(c)], mean_var[:, t, 0:1], gain[:, chunk(c)],
                            ALU.subtract, ALU.mult)) for t in range(TT)]
                        for t in range(TT):
                            step.wait(centred[t])
                            n = nc.vector.scalar_tensor_tensor(dst[:, t, chunk(c)], dst[:, t, chunk(c)], rstd[:, t:t + 1],
                                                               shift[:, chunk(c)], ALU.mult, ALU.add)
                        n.then_inc(rows_ready, 1)
                    if c and k == 0:
                        group_to_lo(name, c - 1, a_hi, a_lo, 4 * (c - 1),
                                    source=silu[:, (c - 1) % 2, :].rearrange("p (k t) -> p k t", t=T))
                    elif c:
                        group_to_lo(name, c - 1, a_hi, a_lo, 4 * (c - 1))

            nc.vector.memset(eps[:, :], EPS).then_inc(pair_free, 1)
            nc.vector.memset(u_pad[:, :, 0:PAD], 0.0).then_inc(pair_free, 1)
            for c in range(CHUNKS):
                group_to_lo("x", c, a_hi, a_lo, 4 * c)
            dve.wait_ge(params_turned, 1)
            link(nc.vector.tensor_copy(params[:, :, 0:TAPS], bank[:, 4, 0:KT * TAPS].rearrange("p (c w) -> p c w", w=TAPS)))
            for n, r in ((TAPS, 2), (TAPS + 1, 0), (TAPS + 2, 1)):
                last = nc.vector.tensor_copy(params[:, :, n], bank[:, 5, r * KT:(r + 1) * KT])
            last.then_inc(params_done, 1)

            two_pi = 2 * np.pi
            part1 = 6.28125
            part2 = float(np.round((two_pi - part1) * 2.0 ** 20) / 2.0 ** 20)
            part3 = float(np.float32(two_pi - part1 - part2))
            magic = 1.5 * 2.0 ** 23
            pi = float(np.nextafter(np.float32(np.pi), np.float32(0)))
            dve.wait_ge(const_landed, 64)
            link(nc.vector.tensor_copy(pos_f[:, :], pos_i[:, :]))
            for t in range(TT):
                link(nc.vector.tensor_scalar(angle[:, t, :], inv_freq[:, :], pos_f[:, t:t + 1], None, ALU.mult))
            for dst, quarter in ((for_cos, 0.25), (for_sin, 0.0)):
                link(nc.vector.tensor_scalar(turns[:, :, :], angle[:, :, :], 1.0 / two_pi, quarter, ALU.mult, ALU.add))
                link(nc.vector.tensor_scalar(turns[:, :, :], turns[:, :, :], magic, magic, ALU.add, ALU.subtract))
                link(nc.vector.scalar_tensor_tensor(dst[:, :, :], turns[:, :, :], -part1, angle[:, :, :], ALU.mult, ALU.add))
                link(nc.vector.scalar_tensor_tensor(dst[:, :, :], turns[:, :, :], -part2, dst[:, :, :], ALU.mult, ALU.add))
                link(nc.vector.scalar_tensor_tensor(dst[:, :, :], turns[:, :, :], -part3, dst[:, :, :], ALU.mult, ALU.add))
                link(nc.vector.tensor_scalar(dst[:, :, :], dst[:, :, :], quarter * two_pi, pi, ALU.add, ALU.min))
                n = nc.vector.tensor_scalar(dst[:, :, :], dst[:, :, :], -pi, None, ALU.max)
                if quarter:
                    link(n)
            n.then_inc(angles_done, 1)
            dve.wait_ge(sines_done, 2)
            link(nc.vector.tensor_scalar(nsin_t[:, :, :], sin_t[:, :, :], -1.0, None, ALU.mult))

            def conv_stats(j):
                dve.wait_ge(conv_stored, j + 1)
                for t in range(TT):
                    mark(nc.vector.bn_stats(stats[:, t, bass.ds(j, 1), :], v_tok[:, t, bass.ds(j * T, T)]))

            def conv_unit(j, half, first=False, second=False):
                if not first:
                    dve.wait_ge(conv_done, 2 * j)
                link(nc.vector.tensor_copy(taps[:, :, :], params[:, bass.ds(2 * j, 2), :]))
                for k in range(2):
                    dve.wait_ge(sig_done, 2 * j + k + 1)
                    n = nc.vector.scalar_tensor_tensor(u_pad[:, k, PAD:PAD + T], pair(half)[:, k, 0:T],
                                                       taps[:, k, TAPS + 1:TAPS + 2], sig[:, k, :], ALU.add, ALU.mult)
                    mark(n) if k == 0 else n.then_inc(pair_free, 1)
                dve.wait_ge(pair_free, j + 3)
                if not (first or second):
                    dve.wait_ge(conv_copied, j - 1)
                marks = [None, None]
                for w in range(TAPS):
                    for k in range(2):
                        acc = bank[:, 4 + half, k * T:(k + 1) * T]
                        u = u_pad[:, k, w:w + T]
                        if w == 0:
                            n = nc.vector.tensor_scalar(acc, u, taps[:, k, 0:1], taps[:, k, TAPS:TAPS + 1], ALU.mult, ALU.add)
                        else:
                            step.wait(marks[k])
                            n = nc.vector.scalar_tensor_tensor(acc, u, taps[:, k, w:w + 1], acc, ALU.mult, ALU.add)
                        if w < TAPS - 1:
                            marks[k] = mark(n)
                        else:
                            n.then_inc(conv_done, 1)

            conv_unit(0, 0, first=True)
            conv_unit(1, 1, second=True)
            rounds = UNITS["conv"] // 2 - 1
            with dve.Fori(0, rounds) as i:
                step.enter(i, 2 * (TT + 2 + 2 * (TAPS - 1)))
                for k in range(2):
                    conv_stats(2 * i + k)
                    conv_unit(2 * i + 2 + k, k)
                step.leave(rounds)
            conv_stats(UNITS["conv"] - 2)
            conv_stats(UNITS["conv"] - 1)
            norm(0, UNITS["conv"], v_tok, v_tok)

            def add_units(stage):
                with dve.Fori(0, UNITS[stage] // 2) as i:
                    step.enter(i, 2 * TT + 2)
                    for k in range(2):
                        u, c = UNIT[stage] + 2 * i + k, 2 * i + k
                        q = QUARTER[stage] + 4 * i + 2 * k
                        splits(q, parity(stage), range(0, 7))
                        dve.wait_ge(used, 4 * q + 8)
                        for t in range(TT):
                            x = x_tok[:, t, bass.ds(c * COLS, COLS)]
                            n = nc.vector.scalar_tensor_tensor(x, x, ALPHA, pair(UNIT[stage] + k)[:, t, :], ALU.mult, ALU.add)
                            mark(n) if t == 0 else n.then_inc(pair_free, 1)
                        dve.wait_ge(pair_free, u + 3)
                        for t in range(TT):
                            mark(nc.vector.bn_stats(stats[:, t, bass.ds(c, 1), :], x_tok[:, t, bass.ds(c * COLS, COLS)]))
                        splits(q, parity(stage), range(7, 8))
                    step.leave(UNITS[stage] // 2)

            def mlp(layer):
                stage = f"mlp{layer}"
                norm(NORMS.index(f"ln1_{layer}"), CHUNKS, x_tok, x_tok)
                group_to_lo(f"p{layer}", 0, p_hi, p_lo, 0, blocks=PLE // P)
                dve.wait_ge(scaled, CHUNKS * (layer + 1))

                def slab(s, last=False):
                    for c in range(2 * CHUNKS):
                        q = QUARTER[stage] + 2 * c + 16 * s
                        u = UNIT[stage] + c + 8 * s
                        splits(q, parity(stage), range(0, 2))
                        if 1 <= c <= CHUNKS:
                            group_to_lo(stage, c - 1, b_hi, b_lo, 4 * (c - 1), off=4 * s)
                        splits(q, parity(stage), range(2, 7))
                        ps = pair(UNIT[stage] + c)
                        for t in range(TT):
                            if c < CHUNKS:
                                dve.wait_ge(relu_done, TT * (CHUNKS * (4 * layer + s) + c) + t + 1)
                                n = nc.vector.tensor_tensor(s_tok[:, t, :], s_tok[:, t, :], ps[:, t, :], ALU.mult)
                            else:
                                dve.wait_ge(used, 4 * q + 8)
                                x = x_tok[:, t, chunk(c - CHUNKS)]
                                n = nc.vector.tensor_tensor(x, x, ps[:, t, :], ALU.add)
                            mark(n) if t == 0 else n.then_inc(pair_free, 1)
                        if c >= CHUNKS and last:
                            dve.wait_ge(pair_free, u + 3)
                            for t in range(TT):
                                mark(nc.vector.bn_stats(stats[:, t, c - CHUNKS, :], x_tok[:, t, chunk(c - CHUNKS)]))
                        splits(q, parity(stage), range(7, 8))

                with dve.Fori(0, F // D - 1) as s:
                    step.enter(s, 2 * CHUNKS)
                    slab(s)
                    step.leave(F // D - 1)
                slab(F // D - 1, last=True)

            def ple(layer):
                proj, gate = f"proj{layer}", f"gate{layer}"
                norm(NORMS.index(f"ln2_{layer}"), CHUNKS, x_tok, x_tok)
                for e in range(4):
                    split_lo(QUARTER[proj] + 2, e, parity(proj))
                for c in range(CHUNKS):
                    q = QUARTER[gate] + 2 * c
                    more = range(PIECES) if layer < DEPTH - 1 or c < CHUNKS - 1 else ()
                    splits(q, parity(gate), more[0:2])
                    if c and layer == 0:
                        group_to_lo(gate, c - 1, b_hi, b_lo, 4 * (c - 1))
                    splits(q, parity(gate), more[2:7])
                    dve.wait_ge(proj_stored, CHUNKS * layer + c + 1)
                    for t in range(TT):
                        dve.wait_ge(gate_done, TT * (CHUNKS * layer + c) + t + 1)
                        n = nc.vector.tensor_tensor(s_tok[:, t, :], s_tok[:, t, :], v_tok[:, t, chunk(c)], ALU.mult)
                        m = mark(n) if t == 0 else n.then_inc(pair_free, 1)
                    dve.wait_ge(pair_free, UNIT[gate] + c + 3)
                    for t in range(TT):
                        n = nc.vector.tensor_tensor(s_tok[:, t, :], s_tok[:, t, :], x_tok[:, t, chunk(c)], ALU.add)
                        if layer == 0:
                            m = mark(n)
                    if layer == 0:
                        step.wait(m)
                        for t in range(TT):
                            n = nc.vector.bn_stats(stats[:, t, c, :], s_tok[:, t, :])
                    n.then_inc(x_new, 1)
                    splits(q, parity(gate), more[7:8])
                if layer == 0:
                    group_to_lo(gate, CHUNKS - 1, b_hi, b_lo, 4 * (CHUNKS - 1))

            def rotate(ps, dst, t):
                def halves(x):
                    return x.rearrange("p (h s f) -> p h s f", s=2, f=HALF)

                def table(x, n):
                    return x[:, t:t + 1, :].broadcast_to([P, n, HALF])

                mark(nc.vector.tensor_tensor(dst.rearrange("p (h f) -> p h f", f=HALF), ps.rearrange("p (h f) -> p h f", f=HALF),
                                             table(cos_t, 2 * HPU), ALU.mult))
                mark(nc.vector.tensor_tensor(halves(rot_tmp[:, :])[:, :, 0, :], halves(ps)[:, :, 1, :], table(nsin_t, HPU), ALU.mult))
                link(nc.vector.tensor_tensor(halves(rot_tmp[:, :])[:, :, 1, :], halves(ps)[:, :, 0, :], table(sin_t, HPU), ALU.mult))
                return nc.vector.tensor_tensor(dst, dst, rot_tmp[:, :], ALU.add)

            def keys_and_values():
                for c in range(CHUNKS + 1):
                    q = QUARTER["kv"] + 2 * c
                    if c:
                        splits(q, parity("kv"), range(0, 3))
                        dve.wait_ge(group_done, GROUP["k"] + c)
                        nc.vector.tensor_copy(k_t[:, HPU * (c - 1):HPU * c, :], group_out(GROUP["k"] + c - 1)).then_inc(group_free, 1)
                    if c == CHUNKS:
                        break
                    splits(q, parity("kv"), range(3 if c else 0, 7))
                    dve.wait_ge(used, 4 * q + 8)
                    link(rotate(pair(UNIT["kv"] + c)[:, 0, :], s_tok[:, 0, :], 0))
                    rotate(pair(UNIT["kv"] + c)[:, 1, :], s_tok[:, 1, :], 1).then_inc(pair_free, 1)
                    dve.wait_ge(pair_free, UNIT["kv"] + c + 3)
                    splits(q, parity("kv"), range(7, 8))
                for c in range(CHUNKS):
                    q = QUARTER["kv"] + 2 * (CHUNKS + c)
                    splits(q, parity("kv"), range(3 if c == 0 else 0, 7))
                    dve.wait_ge(used, 4 * q + 8)
                    for t in range(TT):
                        n = nc.vector.tensor_copy(v_tok[:, t, chunk(c)], pair(UNIT["kv"] + CHUNKS + c)[:, t, :])
                        mark(n) if t == 0 else n.then_inc(pair_free, 1)
                    splits(q, parity("kv"), range(7, 8))

            dve.wait_ge(lo_done, 4 * QUARTER["conv_out"] + PIECES)
            add_units("conv_out")
            mlp(0)
            ple(0)
            norm(NORMS.index("kv_ln"), CHUNKS, x_tok, v_tok)
            keys_and_values()

            def masked_max(h):
                dve.wait_ge(scores_done, h + 1)
                if h >= 2:
                    dve.wait_ge(o_done, h - 1)
                for t, b in ((0, S0), (1, S1)):
                    scores = bank[:, b:b + 2, :].rearrange("p b n -> p (b n)")[:, 0:G * KEYS[t]]
                    mark(nc.vector.tensor_tensor_reduce(out=soft[:, h % 2, seen(t):seen(t, G)], in0=scores,
                                                        in1=mask[:, seen(t):seen(t, G)], scale=SCALE, scalar=MASKED,
                                                        op0=ALU.add, op1=ALU.max, accum_out=row_max[:, h % 2, t:t + 1]))
                step.wait(step.n)
                nc.vector.tensor_scalar(neg_max[:, h % 2, :], row_max[:, h % 2, :], -1.0, None, ALU.mult).then_inc(soft_ready, 1)

            def add_groups(h):
                dve.wait_ge(exp_done, 2 * h + 2)
                mark(nc.vector.reciprocal(row_inv[:, h % 2, :], row_sum[:, h % 2, :]))
                part = [[soft[:, h % 2, seen(t, g):seen(t, g + 1)] for g in range(G)] for t in range(TT)]
                marks = [mark(nc.vector.tensor_tensor(part[t][0], part[t][0], part[t][1], ALU.add)) for t in range(TT)]
                for t in range(TT):
                    step.wait(marks[t])
                    n = nc.vector.tensor_tensor(part[t][0], part[t][0], part[t][2], ALU.add)
                n.then_inc(prob_done, 1)

            def copy_q(i, g, t):
                dve.wait_ge(q_turned, TT * (G * i + g) + t + 1)
                nc.vector.tensor_copy(q_t[:, g, :, t * P:(t + 1) * P],
                                      bank[:, TURN, :].rearrange("p (h t) -> p h t", t=P)).then_inc(q_copied, 1)

            def rotate_q(i, g):
                u = G * i + g
                dve.wait_ge(used, 4 * (QUARTER["q"] + 2 * u) + 8)
                if u:
                    dve.wait_ge(q_turned, TT * u)
                for t in range(TT):
                    n = rotate(pair(UNIT["q"] + u)[:, t, :], q_rot[:, t, :], t)
                    link(n) if t == 0 else n.then_inc(pair_free, 1)
                dve.wait_ge(pair_free, UNIT["q"] + u + 3)

            for i in range(BLOCKS):
                for gap in range(G * PIECES):
                    h = HPU * (i - 1)
                    if gap in ROTATE and (i or gap):
                        rotate_q(i - (gap == 0), ROTATE[gap])
                    if gap in TURN_Q and (i or gap > 3):
                        copy_q(i - (gap <= 3), *TURN_Q[gap])
                    if i and gap in SCORES:
                        masked_max(h + SCORES[gap])
                    if i and gap - 1 in SCORES:
                        add_groups(h + SCORES[gap - 1])
                    q = QUARTER["q"] + 2 * (G * i + gap // PIECES)
                    split_lo(q + 2, gap % PIECES, parity("q"))
            rotate_q(BLOCKS - 1, G - 1)
            copy_q(BLOCKS - 1, G - 1, 0)
            copy_q(BLOCKS - 1, G - 1, 1)
            for h in range(HEADS - HPU, HEADS):
                masked_max(h)
                add_groups(h)
            for c in range(CHUNKS):
                group_to_lo("o", c, b_hi, b_lo, 4 * c)
            add_units("attn_out")
            mlp(1)
            ple(1)

        @block.tensor
        def _(pe):
            def products(q, e, turned, hi, lo, kt, ps, first, last, done=None):
                slot = (e + turned) % PIECES
                pe.wait_ge(lo_done, 4 * q + e + 1)
                for k in range(KP):
                    for t in range(TT):
                        x_hi, x_lo = (x[:, kt + k, t * P:(t + 1) * P] for x in (hi, lo))
                        for n, (x, w) in enumerate(((x_hi, w_hi), (x_hi, w_lo), (x_lo, w_hi))):
                            ins = nc.tensor.matmul(ps[:, t, :], x, w[:, slot, k, :], start=first and k == 0 and n == 0,
                                                   stop=last and k == KP - 1 and n == 2)
                ins.then_inc(used, 1)

            def unit(q, u, turned, hi, lo, ps, ready=None, between=None, free=True):
                for e in range(PIECES):
                    if between is not None:
                        between(e)
                    if e == 0 and free:
                        pe.wait_ge(pair_free, u + 1)
                    if ready is not None and e % 2 == 0:
                        ready(e // 2)
                    products(q, e, turned, hi, lo, KP * e, ps, e == 0, e == PIECES - 1)

            def split_wait(stage, off=0):
                def ready(c):
                    pe.wait_ge(group_free, GROUP[stage] + c + 1 + off)
                return ready

            def turn_group(g, src, off=0, cols=0, blocks=4):
                if g >= 2:
                    pe.wait_ge(group_free, g - 1 + off)
                dst = group_out(g)
                for k in range(blocks):
                    for t in range(TT):
                        n = nc.tensor.transpose(dst[:, k, t * P:(t + 1) * P], src[:, t, cols + k * P:cols + (k + 1) * P], ident[:, :])
                n.then_inc(group_done, 1)

            def turn_norm(name, c, src):
                pe.wait_ge(rows_ready, ROWS[name] + c + 1)
                turn_group(GROUP[name] + c, src, cols=c * COLS)

            pe.wait_ge(const_landed, 64)
            for c in range(CHUNKS):
                pe.wait_ge(x_landed[c], 16)
                turn_group(GROUP["x"] + c, x_tok, cols=c * COLS)

            def turn_params():
                pe.wait_ge(rows_landed, 48)
                pe.wait_ge(group_free, GROUP["x"] + 3)
                for c in range(KT):
                    nc.tensor.transpose(bank[:, 4, c * TAPS:(c + 1) * TAPS], dw_rows[:, c * P:(c + 1) * P], ident[0:TAPS, 0:TAPS])
                nc.tensor.transpose(bank[:, 5, 0:3 * KT], bias_rows[:, :], ident[0:3 * KT, 0:3 * KT]).then_inc(params_turned, 1)

            def conv_turn(j, half):
                pe.wait_ge(conv_copied, j + 1)
                for t in range(TT):
                    for k in range(2):
                        n = nc.tensor.transpose(bank[:, 6 + half, t * T + k * P:t * T + (k + 1) * P], c_copy[:, k, t * P:(t + 1) * P], ident[:, :])
                n.then_inc(conv_turned, 1)

            def conv_unit(j, q, half, turn=None):
                pe.wait_ge(pair_free, j + 1)
                for e in range(PIECES):
                    if e == 3 and turn is not None:
                        turn()
                    if e % 2 == 0:
                        split_wait("x")(e // 2)
                    pe.wait_ge(lo_done, 4 * q + e + 1)
                    side = e % 2
                    for k in range(2 * KP):
                        kt = 2 * KP * (e // 2) + k
                        for b in range(2):
                            cols = slice(k % 2 * T + b * P, k % 2 * T + (b + 1) * P)
                            ws = [w[:, e, k // 2, cols] for w in (w_hi, w_lo)]
                            xs = [x[:, kt, :] for x in (a_hi, a_lo)]
                            for n, (w, x) in enumerate(((ws[0], xs[0]), (ws[1], xs[0]), (ws[0], xs[1]))):
                                ins = nc.tensor.matmul(pair(half)[:, b, side * T:(side + 1) * T], w, x,
                                                       start=kt == 0 and side == 0 and n == 0,
                                                       stop=kt == KT - 1 and n == 2, skip_group_check=True)
                    ins.then_inc(used, 1)

            conv_unit(0, 0, 0, turn=turn_params)
            conv_unit(1, 2, 1)
            with pe.Fori(1, UNITS["conv"] // 2) as i:
                for k in range(2):
                    j = 2 * i + k
                    conv_unit(j, 2 * j, k, turn=lambda: conv_turn(j - 2, k))
            conv_turn(UNITS["conv"] - 2, 0)
            conv_turn(UNITS["conv"] - 1, 1)
            for c in range(CHUNKS):
                turn_norm("conv_ln", c, v_tok)

            def plain_units(stage, hi, lo, group):
                with pe.Fori(0, UNITS[stage] // 2) as i:
                    for k in range(2):
                        unit(QUARTER[stage] + 4 * i + 2 * k, UNIT[stage] + 2 * i + k, parity(stage), hi, lo,
                             pair(UNIT[stage] + k), ready=split_wait(group) if k == 0 else None)

            def mlp(layer):
                stage = f"mlp{layer}"
                for c in range(CHUNKS):
                    turn_norm(f"ln1_{layer}", c, x_tok)
                pe.wait_ge(p_landed, 16 * (layer + 1))
                turn_group(GROUP[f"p{layer}"], p_tok, blocks=PLE // P)
                with pe.Fori(0, F // D) as s:
                    for c in range(2 * CHUNKS):
                        q, u = QUARTER[stage] + 2 * c + 16 * s, UNIT[stage] + c + 8 * s

                        def between(e):
                            if e == 2 and 1 <= c <= CHUNKS:
                                pe.wait_ge(pair_free, u + 2)
                                turn_group(GROUP[stage] + c - 1, s_tok, off=4 * s)

                        if c < CHUNKS:
                            ready = split_wait(f"ln1_{layer}") if c == 0 else None
                        else:
                            ready = split_wait(stage, off=4 * s) if c == CHUNKS else None
                        x = (a_hi, a_lo) if c < CHUNKS else (b_hi, b_lo)
                        unit(q, u, parity(stage), *x, pair(UNIT[stage] + c), ready=ready, between=between)

            def ple(layer):
                proj, gate, name = f"proj{layer}", f"gate{layer}", f"ln2_{layer}"
                pe.wait_ge(pair_free, UNIT[gate] + 2)
                pe.wait_ge(group_free, GROUP[f"p{layer}"] + 1)
                for c in range(CHUNKS):
                    if c >= 2:
                        pe.wait_ge(proj_stored, CHUNKS * layer + c - 1)
                        turn_norm(name, c - 2, x_tok)
                    slot = (c + parity(proj)) % PIECES
                    pe.wait_ge(lo_done, 4 * QUARTER[proj] + c + 1)
                    for t in range(TT):
                        for k in range(KP):
                            x_hi, x_lo = (x[:, k, t * P:(t + 1) * P] for x in (p_hi, p_lo))
                            for n, (x, w) in enumerate(((x_hi, w_hi), (x_hi, w_lo), (x_lo, w_hi))):
                                ins = nc.tensor.matmul(pair(c)[:, t, :], x, w[:, slot, k, :], start=k == 0 and n == 0,
                                                       stop=k == KP - 1 and n == 2)
                    ins.then_inc(used, 1)
                turn_norm(name, 2, x_tok)
                turn_norm(name, 3, x_tok)
                pe.wait_ge(proj_stored, CHUNKS * (layer + 1))
                for c in range(CHUNKS):
                    def between(e):
                        if e == 2 and c and layer == 0:
                            turn_gate(c - 1)
                    unit(QUARTER[gate] + 2 * c, UNIT[gate] + c, parity(gate), a_hi, a_lo, pair(UNIT[gate] + c),
                         ready=split_wait(name) if c == 0 else None, between=between)
                if layer == 0:
                    turn_gate(CHUNKS - 1)

            def turn_gate(c):
                pe.wait_ge(x_new, c + 1)
                turn_group(GROUP["gate0"] + c, s_tok)

            plain_units("conv_out", a_hi, a_lo, "conv_ln")
            mlp(0)
            ple(0)

            for c in range(CHUNKS):
                turn_norm("kv_ln", c, v_tok)

            def kv_between(c):
                def between(e):
                    if e == 3 and 1 <= c <= CHUNKS:
                        pe.wait_ge(pair_free, UNIT["kv"] + c + 2)
                        turn_group(GROUP["k"] + c - 1, s_tok)
                return between

            for c in range(2 * CHUNKS):
                unit(QUARTER["kv"] + 2 * c, UNIT["kv"] + c, parity("kv"), a_hi, a_lo, pair(UNIT["kv"] + c),
                     ready=split_wait("kv_ln") if c == 0 else None, between=kv_between(c))

            def scores(h):
                hh = h % HPU
                if h % HPU == 0:
                    pe.wait_ge(q_copied, TT * G * (h // HPU + 1))
                if h:
                    pe.wait_ge(soft_ready, h)
                    pe.wait_ge(o_stored, TT * h)
                for g in range(G):
                    nc.tensor.matmul(bank[:, S0, g * P:(g + 1) * P], q_t[:, g, hh, 0:P], k_t[:, h, 0:P], start=True, stop=True)
                for g in range(G):
                    n = nc.tensor.matmul(bank[:, S1 + g // 2, (g % 2) * T:(g % 2 + 1) * T], q_t[:, g, hh, P:T], k_t[:, h, :],
                                         start=True, stop=True)
                n.then_inc(scores_done, 1)

            def turn_probs(h, copied):
                pe.wait_ge(prob_done, h + 1)
                if copied:
                    pe.wait_ge(q_copied, copied)
                if h:
                    pe.wait_ge(prob_copied, h)
                part = [soft[:, h % 2, seen(t):seen(t, 1)] for t in range(TT)]
                nc.tensor.transpose(bank[:, TURN, 0:P], part[0], ident[:, :])
                nc.tensor.transpose(bank[:, TURN, P:2 * P], part[1][:, 0:P], ident[:, :])
                nc.tensor.transpose(bank[:, TURN, 2 * P:3 * P], part[1][:, P:T], ident[:, :]).then_inc(prob_turned, 1)

            def outputs(h):
                pe.wait_ge(prob_copied, h + 1)
                p_t = prob_t(h % 2)
                cols = slice(h * HD, (h + 1) * HD)
                nc.tensor.matmul(bank[:, S0, 0:HD], p_t[:, 0:P], v_tok[:, 0, cols], start=True, stop=True)
                nc.tensor.matmul(bank[:, S0, HD:2 * HD], p_t[:, P:2 * P], v_tok[:, 0, cols], start=True, stop=False)
                nc.tensor.matmul(bank[:, S0, HD:2 * HD], p_t[:, 2 * P:3 * P], v_tok[:, 1, cols], start=False, stop=True) \
                  .then_inc(o_done, 1)

            turned = [0]

            def turn_q(i, g, t, probs):
                pe.wait_ge(pair_free, UNIT["q"] + G * i + g + 3)
                if turned[0]:
                    pe.wait_ge(q_copied, turned[0])
                if probs:
                    pe.wait_ge(prob_copied, probs)
                for hh in range(HPU):
                    n = nc.tensor.transpose(bank[:, TURN, hh * P:(hh + 1) * P], q_rot[:, t, hh * HD:(hh + 1) * HD], ident[:, :])
                n.then_inc(q_turned, 1)
                turned[0] += 1

            def q_between(i, g):
                def between(e):
                    gap, h = g * PIECES + e, HPU * (i - 1)
                    if gap in TURN_Q and (i or gap > 3):
                        probs = h + sum(x < gap for x in TURN_P) if i else 0
                        turn_q(i - (gap <= 3), *TURN_Q[gap], probs)
                    if i and gap in SCORES:
                        scores(h + SCORES[gap])
                    if i and gap in TURN_P:
                        turn_probs(h + TURN_P[gap], turned[0])
                    if i and gap in PV:
                        outputs(h + PV[gap])
                return between

            for i in range(BLOCKS):
                for g in range(G):
                    u = G * i + g
                    unit(QUARTER["q"] + 2 * u, UNIT["q"] + u, parity("q"), b_hi, b_lo, pair(UNIT["q"] + u), between=q_between(i, g))
            last = HEADS - HPU
            turn_q(BLOCKS - 1, G - 1, 0, last)
            turn_q(BLOCKS - 1, G - 1, 1, last)
            for h in range(last, HEADS):
                scores(h)
                turn_probs(h, turned[0])
                outputs(h)
            pe.wait_ge(o_stored, TT * HEADS)
            for c in range(CHUNKS):
                turn_group(GROUP["o"] + c, o_tok, cols=c * COLS)
            plain_units("attn_out", b_hi, b_lo, "o")
            mlp(1)
            ple(1)


_INS = ("x", "p", "positions", "conv_w_in", "conv_b_in", "conv_dw", "conv_dw_b", "conv_ln_g", "conv_ln_b",
        "conv_w_out", "kv_ln_g", "kv_ln_b", "w_kv", "attn_w_q", "attn_w_o", "ln1_g", "ln1_b", "mlp_up",
        "mlp_down", "ln2_g", "ln2_b", "ple_proj", "ple_gate")


def shape_constants():
    freq = 10000.0 ** (-np.arange(HALF, dtype=np.float32) * np.float32(2.0 / HD))
    parts = [np.eye(P), np.broadcast_to(freq, (P, HALF))]
    for t, keys in enumerate(KEYS):
        back = (t * P + np.arange(P))[:, None] - np.arange(keys)[None, :]
        for window, dilation in WINDOWS:
            inside = (back >= 0) & (back <= window) & (back % dilation == 0)
            parts.append(np.where(inside, 0.0, MASKED))
    return np.ascontiguousarray(np.concatenate(parts, axis=1).astype(np.float32))


def kernel(**inputs):
    import concourse.bacc as bacc
    from concourse.bass_utils import run_bass_kernel_spmd

    nc = bacc.Bacc("TRN2", target_bir_lowering=False, num_devices=1)
    arrays, args = {}, {}
    for name in _INS + ("consts",):
        a = shape_constants() if name == "consts" else np.ascontiguousarray(inputs[name])
        arrays[f"in_{name}"] = a
        args[name] = nc.dram_tensor(f"in_{name}", a.shape, mybir.dt.from_np(a.dtype), kind="ExternalInput").ap()
    out = nc.dram_tensor("out", (1, T, D), F32, kind="ExternalOutput").ap()
    trunk(nc, args, out)
    result = run_bass_kernel_spmd(nc, [arrays], core_ids=[0])
    return result.results[0]["out"]
```

```python
from contextlib import ExitStack

import numpy as np

import concourse.bass as bass
from concourse import mybir

F32 = mybir.dt.float32
F32R = mybir.dt.float32r
BF16 = mybir.dt.bfloat16
I32 = mybir.dt.int32
ALU = mybir.AluOpType
ACT = mybir.ActivationFunctionType

P = 128
D = 2048
T = 256
TT = T // P
KT = D // P
F = 4 * D
COLS = 512
CHUNKS = D // COLS
PIECES = 8
KP = KT // PIECES
RAW = 4
TAPS = 31
PAD = TAPS - 1
PE_TAPS = 3
LAST_PE_TAPS = 15
HD = 128
HALF = HD // 2
HEADS = D // HD
HPU = COLS // HD
WINDOWS = ((128, 1), (512, 4), (2048, 16))
G = len(WINDOWS)
PLE = 256
DEPTH = 2
ALPHA = float((2 * DEPTH) ** 0.25)
EPS = 1e-5
SCALE = float(HD) ** -0.5
MASKED = -3.0e38
KEYS = (P, T)
PARAMS = TAPS + 3

UNITS = dict(conv=8, conv_out=4, mlp0=32, proj0=0, gate0=4, kv=8, q=12, attn_out=4, mlp1=32, proj1=0, gate1=4)
UNIT, QUARTER, GROUP, HIGH, ROWS = {}, {}, {}, {}, {}
_u = _q = 0
for _s, _n in UNITS.items():
    UNIT[_s], QUARTER[_s] = _u, _q
    _u += _n
    _q += 2 * _n if _n else 1
NORMS = ("conv_ln", "ln1_0", "ln2_0", "kv_ln", "ln1_1", "ln2_1")
ALL = TT * CHUNKS
_g = _h = _r = 0
for _s, _n in (("x", ALL), ("conv_ln", ALL), ("ln1_0", ALL), ("p0", TT), ("mlp0", 4 * ALL), ("ln2_0", ALL),
               ("gate0", ALL), ("kv_ln", ALL), ("k", ALL), ("o", ALL), ("ln1_1", ALL), ("p1", TT),
               ("mlp1", 4 * ALL), ("ln2_1", ALL)):
    GROUP[_s], HIGH[_s], ROWS[_s] = _g, _h, _r
    _g += _n
    _h += _n if _s != "k" else 0
    _r += _n if _s in NORMS else 0


def norm_group(name, t, c):
    return CHUNKS * t + c + (-TT if name == "kv_ln" and t == 0 else 0)


def gate_group(t, c):
    return TT * c + t + (CHUNKS if c == CHUNKS - 1 else 0)


def taken(u, t):
    return TT * u + t + 1


SCORES = {4 + 4 * n: n for n in range(HPU)}
TURN_P = {6 + 4 * n: n for n in range(HPU)}
PV = {7 + 4 * n: n for n in range(HPU)}
ROTATE = {0: (2, 0), 1: (2, 1), 10: (0, 0), 14: (0, 1), 18: (1, 0), 20: (1, 1)}
TURN_Q = {2: (2, 0), 3: (2, 1), 17: (0, 0), 19: (0, 1), 21: (1, 0), 23: (1, 1)}
BLOCKS = HEADS // HPU
LAST = HEADS - HPU

FIRST = ((1, 4), (1, 5), (1, 6), (1, 7))
EAGER = ((0, 0), (0, 0), (0, 2), (0, 4))
SOON = ((1, 0), (1, 1), (1, 2), (1, 4))
LATER = ((0, 6), (0, 7), (1, 0), (1, 1))


class Count:

    def __init__(self, engine, sem):
        self.engine, self.sem, self.n, self.off = engine, sem, 0, 0

    def mark(self, instruction):
        instruction.then_inc(self.sem, 1)
        self.n += 1
        return self.n

    def wait(self, value):
        self.engine.wait_ge(self.sem, self.off + value)

    def link(self, instruction):
        self.wait(self.mark(instruction))

    def enter(self, i, by):
        self.off, self.by, self.at = i * by, by, self.n

    def leave(self, rounds):
        assert self.n - self.at == self.by, (self.n - self.at, self.by)
        self.off, self.n = 0, self.at + self.by * rounds


def trunk(nc, A, out):
    with ExitStack() as ctx:
        place = {"at": -(-nc.sbuf_base // 32) * 32}

        def region(nbytes):
            here = place["at"]
            place["at"] = here + -(-nbytes // 8) * 8
            return here

        def at(name, shape, dt, offset):
            return nc.alloc_sbuf_tensor_at(name, shape, dt, offset=offset, align_bytes=8)

        def small(name, shape, dt=F32):
            return at(name, shape, dt, region(int(np.prod(shape[1:])) * 4))

        PIECE = KP * COLS * 4
        SPLIT = KT * T * 4
        raw = at("raw", [P, RAW, KP, COLS], F32, region(RAW * PIECE))
        w_hi = at("w_hi", [P, PIECES, KP, COLS], F32R, region(PIECES * PIECE))
        w_lo = at("w_lo", [P, PIECES, KP, COLS], F32R, region(PIECES * PIECE))

        r_a = region(2 * SPLIT)
        a_hi = at("a_hi", [P, KT, T], F32R, r_a)
        a_lo = at("a_lo", [P, KT, T], F32R, r_a + SPLIT)
        o_tok = at("o_tok", [P, TT, D], F32, r_a)
        q_t = at("q_t", [P, G, HPU, T], F32, r_a + SPLIT)
        q_rot = at("q_rot", [P, TT, COLS], F32, r_a + SPLIT + G * HPU * T * 4)

        r_b = region(2 * SPLIT)
        b_hi = at("b_hi", [P, KT, T], F32R, r_b)
        b_lo = at("b_lo", [P, KT, T], F32R, r_b + SPLIT)
        params = at("params", [P, KT, PARAMS], F32, r_b)
        dw_rows = at("dw_rows", [TAPS, D], F32, r_b + 4096)
        bias_rows = at("bias_rows", [3 * KT, P], F32, r_b + 4096 + D * 4)
        diag = at("diag", [P, 2, LAST_PE_TAPS, P], F32, r_b + 4096)
        mask_f = at("mask_f", [P, G * sum(KEYS)], F32, r_b + SPLIT + 8192)

        r_g = region(2 * D * 4)
        gain = at("gain", [P, D], F32, r_g)
        shift = at("shift", [P, D], F32, r_g + D * 4)
        k_t = at("k_t", [P, HEADS, T], F32, r_g)

        r_v = region(TT * D * 4)
        v_tok = at("v_tok", [P, TT, D], F32, r_v)
        inv_freq = at("inv_freq", [P, HALF], F32, r_v)
        angle = at("angle", [P, TT, HALF], F32, r_v + 1024)
        turns = at("turns", [P, TT, HALF], F32, r_v + 2048)
        for_cos = at("for_cos", [P, TT, HALF], F32, r_v + 3072)
        for_sin = at("for_sin", [P, TT, HALF], F32, r_v + 4096)

        pos_i = at("pos_i", [P, TT], I32, r_v + 5120)
        pos_f = at("pos_f", [P, TT], F32, r_v + 5152)

        x_tok = small("x_tok", [P, TT, D])

        r_s = region(2 * G * sum(KEYS) * 4)
        s_tok = at("s_tok", [P, TT, COLS], F32, r_s)
        p_hi = at("p_hi", [P, PLE // P, T], F32R, r_s + 4096)
        p_lo = at("p_lo", [P, PLE // P, T], F32R, r_s + 6144)
        silu = at("silu", [P, 2, 4, P], F32, r_s)
        u_pad = at("u_pad", [P, 2, PAD + T], F32, r_s)
        sig = at("sig", [P, 2, T], F32, r_s + 2304)
        c_copy = at("c_copy", [P, 2, T], F32, r_s + 4352)
        taps = at("taps", [P, 2, PARAMS], F32, r_s + 6400)
        soft = at("soft", [P, 2, G * sum(KEYS)], F32, r_s)

        mask = at("mask", [P, G * sum(KEYS)], BF16, region(G * sum(KEYS) * 2))
        ident = small("ident", [P, P])
        cos_t = small("cos_t", [P, TT, HALF])
        sin_t = small("sin_t", [P, TT, HALF])
        nsin_t = small("nsin_t", [P, TT, HALF])
        r_rot = region(COLS * 4)
        rot_tmp = at("rot_tmp", [P, COLS], F32, r_rot)
        p_tok = at("p_tok", [P, TT, PLE], F32, r_rot)
        stats = small("stats", [P, TT, 8, 6])
        mean_var = small("mean_var", [P, TT, 2])
        std = small("std", [P, TT])
        rstd = small("rstd", [P, TT])
        row_max = small("row_max", [P, 2, TT])
        neg_max = small("neg_max", [P, 2, TT])
        row_sum = small("row_sum", [P, 2, TT])
        row_inv = small("row_inv", [P, 2, TT])
        eps = small("eps", [P, 1])
        unused = small("unused", [P, 1])
        assert place["at"] <= nc.sbuf_top, (place["at"], nc.sbuf_top)

        bank = ctx.enter_context(nc.psum_tensor("bank", [P, 8, COLS], F32))

        def pair(n):
            return bank[:, 2 * (n % 2):2 * (n % 2) + 2, :]

        def group_out(g):
            return bank[:, 4 + g % 4, :].rearrange("p (k t) -> p k t", t=P)

        def tile(t):
            return slice(t * P, (t + 1) * P)

        def first_bank(h):
            return 0 if h > LAST and h % 2 else 4

        def head_bank(h, n):
            return bank[:, first_bank(h) + n, :]

        def scores_1(h, g):
            return head_bank(h, g // 2)[:, g % 2 * T:(g % 2 + 1) * T]

        def all_scores(h, t):
            first = first_bank(h)
            if t == 0:
                return bank[:, first + 2, 0:G * P]
            return bank[:, first:first + 2, :].rearrange("p b n -> p (b n)")[:, 0:G * T]

        def scores_0(h, g):
            return head_bank(h, 2)[:, g * P:(g + 1) * P]

        def output(h, t):
            return head_bank(h, 1)[:, T + t * HD:T + (t + 1) * HD]

        def turned_probs(h):
            return head_bank(h, 3)

        TURN = 7

        def sem(name):
            return ctx.enter_context(nc.semaphore(name))

        landed = [sem(f"landed{i}") for i in range(RAW)]
        hi_done = sem("hi_done")
        lo_done = sem("lo_done")
        used = sem("used")
        first_done = sem("first_done")
        tile_free = sem("tile_free")
        x_landed = [sem(f"x_landed{i}") for i in range(CHUNKS)]
        ident_landed = sem("ident_landed")
        const_landed = sem("const_landed")
        rows_landed = sem("rows_landed")
        p_landed = sem("p_landed")
        gain_landed = sem("gain_landed")
        params_turned = sem("params_turned")
        params_done = sem("params_done")
        angles_done = sem("angles_done")
        sines_done = sem("sines_done")
        mask_done = sem("mask_done")
        rows_ready = sem("rows_ready")
        group_done = sem("group_done")
        group_hi = sem("group_hi")
        group_free = sem("group_free")
        sig_done = sem("sig_done")
        conv_done = sem("conv_done")
        diag_done = sem("diag_done")
        taps_added = sem("taps_added")
        conv_copied = sem("conv_copied")
        conv_turned = sem("conv_turned")
        conv_stored = sem("conv_stored")
        relu_done = sem("relu_done")
        var_done = sem("var_done")
        std_done = sem("std_done")
        scaled = sem("scaled")
        proj_stored = sem("proj_stored")
        gate_done = sem("gate_done")
        x_new = sem("x_new")
        x_kept = sem("x_kept")
        q_rotated = sem("q_rotated")
        q_turned = sem("q_turned")
        q_copied = sem("q_copied")
        scores_done = sem("scores_done")
        soft_ready = sem("soft_ready")
        exp_done = sem("exp_done")
        prob_done = sem("prob_done")
        prob_turned = sem("prob_turned")
        prob_copied = sem("prob_copied")
        o_done = sem("o_done")
        o_stored = sem("o_stored")
        act_step = sem("act_step")
        dve_step = sem("dve_step")
        stored = [sem(f"stored{t}") for t in range(TT)]

        def rows(w):
            return w.rearrange("(kt p) n -> p kt n", p=P)

        w_in, w_conv, w_kv, w_q, w_o = (rows(w) for w in (A["conv_w_in"][0], A["conv_w_out"][0], A["w_kv"], A["attn_w_q"][0], A["attn_w_o"][0]))
        w_up = [rows(A["mlp_up"][n]) for n in range(DEPTH)]
        w_down = [rows(A["mlp_down"][n]) for n in range(DEPTH)]
        w_proj = [rows(A["ple_proj"][n]) for n in range(DEPTH)]
        w_gate = [rows(A["ple_gate"][n]) for n in range(DEPTH)]
        x_rows = A["x"][0].rearrange("(t p) n -> p t n", p=P)
        out_rows = out[0].rearrange("(t p) n -> p t n", p=P)
        norm_rows = [(A["conv_ln_g"][0:1, :], A["conv_ln_b"][0:1, :]),
                     (A["ln1_g"][0:1, :], A["ln1_b"][0:1, :]), (A["ln2_g"][0:1, :], A["ln2_b"][0:1, :]),
                     tuple(A[n].rearrange("(a n) -> a n", a=1) for n in ("kv_ln_g", "kv_ln_b")),
                     (A["ln1_g"][1:2, :], A["ln1_b"][1:2, :]), (A["ln2_g"][1:2, :], A["ln2_b"][1:2, :])]

        def chunk(c):
            return slice(c * COLS, (c + 1) * COLS)

        def parity(stage):
            return 4 * (QUARTER[stage] % 2)

        AFTER = {}
        for before, name, after in (("conv_out", "ln1_0", "mlp0"), ("mlp0", "ln2_0", "proj0"), ("gate0", "kv_ln", "kv"),
                                    ("attn_out", "ln1_1", "mlp1"), ("mlp1", "ln2_1", "proj1")):
            AFTER[name] = QUARTER[after], parity(before)

        def seen(t, g=0):
            return G * sum(KEYS[:t]) + g * KEYS[t]

        def prob_t(b):
            return soft[:, b, seen(1, 1):seen(1, 1) + sum(KEYS)]

        block = ctx.enter_context(nc.Block())

        @block.sync
        def _(sp):
            def piece(source, q, e, first=False):
                dst = raw[:, e % RAW, :, :]
                if source.shape[1] != KP:
                    dst = dst.rearrange("p k (h n) -> p (k h) n", h=2)
                if not first:
                    sp.wait_ge(lo_done, 4 * q + e - (RAW - 1))
                sp.dma_start(dst, source).then_inc(landed[e % RAW], 16)

            def unit(w, q, col, row=0):
                for e in range(PIECES):
                    piece(w[:, bass.ds(row + KP * e, KP), bass.ds(col, COLS)], q, e)

            def units(w, stage, n):
                with sp.Fori(0, n) as i:
                    unit(w, QUARTER[stage] + 2 * i, i * COLS)

            def mlp(layer):
                q0 = QUARTER[f"mlp{layer}"]
                with sp.Fori(0, F // D) as s:
                    for c in range(CHUNKS):
                        unit(w_up[layer], q0 + 2 * c + 16 * s, s * D + c * COLS)
                    for c in range(CHUNKS):
                        unit(w_down[layer], q0 + 8 + 2 * c + 16 * s, c * COLS, row=s * KT)

            def ple(layer):
                for c in range(CHUNKS):
                    piece(w_proj[layer][:, :, chunk(c)], QUARTER[f"proj{layer}"], c)
                units(w_gate[layer], f"gate{layer}", CHUNKS)

            def conv_piece(i, e, first=False):
                rows_ = slice(2 * KP * (e // 2), 2 * KP * (e // 2 + 1))
                piece(w_in[:, rows_, bass.ds(i * (COLS // 2) + e % 2 * D, COLS // 2)], 2 * i, e, first)

            for e in range(PIECES):
                conv_piece(0, e, first=e < RAW)
            with sp.Fori(1, UNITS["conv"]) as i:
                for e in range(PIECES):
                    conv_piece(i, e)
            units(w_conv, "conv_out", 4)
            mlp(0)
            ple(0)
            units(w_kv, "kv", 8)
            with sp.Fori(0, BLOCKS) as i:
                for g in range(G):
                    unit(w_q, QUARTER["q"] + 2 * g + 2 * G * i, g * D + i * COLS)
            units(w_o, "attn_out", 4)
            mlp(1)
            ple(1)
            for t in range(TT):
                sp.wait_ge(stored[t], 16 * CHUNKS)

        @block.gpsimd
        def _(pool):
            pool.dma_start(ident[:, :], A["consts"][:, 0:P]).then_inc(ident_landed, 16)
            pool.dma_start(dw_rows[:, :], A["conv_dw"][0].rearrange("w a n -> w (a n)")).then_inc(rows_landed, 16)
            pool.dma_start(bias_rows[0:2 * KT, :], A["conv_b_in"][0].rearrange("(r n) -> r n", n=P)).then_inc(rows_landed, 16)
            pool.dma_start(bias_rows[2 * KT:3 * KT, :], A["conv_dw_b"][0].rearrange("(r n) -> r n", n=P)).then_inc(rows_landed, 16)
            pool.dma_start(inv_freq[:, :], A["consts"][:, P:P + HALF]).then_inc(const_landed, 16)
            pool.dma_start(mask_f[:, :], A["consts"][:, P + HALF:]).then_inc(const_landed, 16)
            with nc.allow_non_contiguous_dma(reason="256 numbers"):
                pool.dma_start(pos_i[:, :], A["positions"].rearrange("b (t p) -> p (b t)", p=P)).then_inc(const_landed, 16)

            def load_gains(k):
                for dst, row in zip((gain, shift), norm_rows[k]):
                    pool.dma_start(dst[:, :], row.partition_broadcast(P)).then_inc(gain_landed, 16)

            def load_p(layer):
                pool.dma_start(p_tok[:, :, :], A["p"][layer, 0].rearrange("(t p) n -> p t n", p=P)).then_inc(p_landed, 16)

            def split_lo(q, e, turned=0):
                slot = (e + turned) % PIECES
                pool.wait_ge(hi_done, 4 * q + e + 1)
                nc.gpsimd.tensor_tensor(w_lo[:, slot, :, :], raw[:, e % RAW, :, :], w_hi[:, slot, :, :],
                                        ALU.subtract).then_inc(lo_done, 1)

            load_gains(0)
            load_p(0)
            with pool.Fori(0, UNITS["conv"] + 1) as i:
                for e in range(PIECES):
                    split_lo(2 * i, e)
            for k, name in enumerate(NORMS[1:], 1):
                if name == "ln1_1":
                    pool.wait_ge(soft_ready, HEADS)
                    load_p(1)
                else:
                    pool.wait_ge(rows_ready, ROWS[NORMS[k - 1]] + ALL)
                load_gains(k)
                q, turned = AFTER[name]
                pool.wait_ge(lo_done, 4 * q)
                for e in range(RAW):
                    split_lo(q, e, turned)

        @block.scalar
        def _(act):
            step = Count(act, act_step)

            def split_hi(q, e, turned, first=False):
                slot = (e + turned) % PIECES
                act.wait_ge(landed[e % RAW], 16 * (q + e // RAW) + 16)
                if not first:
                    act.wait_ge(used, 4 * q + e - (PIECES - 1))
                nc.scalar.activation(w_hi[:, slot, :, :], raw[:, e % RAW, :, :], ACT.Copy).then_inc(hi_done, 1)

            def splits(q, turned, pieces):
                for e in pieces:
                    split_hi(q + 2, e, turned)

            def group_to_hi(g, t, dst, kt, off=0, blocks=4):
                act.wait_ge(group_done, off + g + 1)
                nc.scalar.activation(dst[:, kt:kt + blocks, tile(t)], group_out(g)[:, 0:blocks, :], ACT.Copy).then_inc(group_hi, 1)

            def deviations(k, t):
                act.wait_ge(var_done, TT * k + t + 1)
                nc.scalar.activation(std[:, t:t + 1], mean_var[:, t, 1:2], ACT.Sqrt, bias=eps[:, 0:1]).then_inc(std_done, 1)

            def norm_to_hi(k, t):
                for c in range(CHUNKS):
                    g = GROUP[NORMS[k]] + norm_group(NORMS[k], t, c)
                    if k == 0:
                        act.wait_ge(group_done, g + 1)
                        if CHUNKS * t + c >= 2:
                            act.wait_ge(group_free, g - 1)
                        step.link(nc.scalar.activation(silu[:, g % 2, :, :], group_out(g), ACT.Silu))
                        nc.scalar.activation(a_hi[:, 4 * c:4 * c + 4, tile(t)], silu[:, g % 2, :, :], ACT.Copy).then_inc(group_hi, 1)
                    else:
                        group_to_hi(g, t, a_hi, 4 * c)

            def last_unit(k, q, turned, evacuate=lambda t: None, extra=lambda: None, late=0, store=None):
                evacuate(0)
                deviations(k, 0)
                splits(q, turned, range(0, 3))
                norm_to_hi(k, 0)
                splits(q, turned, range(3, RAW))
                splits(q, turned, range(RAW, RAW + late))
                evacuate(1)
                splits(q, turned, range(RAW + late, PIECES - 1))
                if store is not None:
                    store(0)
                splits(q, turned, range(PIECES - 1, PIECES))
                extra()
                deviations(k, 1)
                if store is not None:
                    for c in range(1, CHUNKS):
                        store(c)
                    splits(q + 2, turned, range(0, 4))
                norm_to_hi(k, 1)

            for c in range(CHUNKS):
                act.dma_start(x_tok[:, :, chunk(c)], x_rows[:, :, chunk(c)]).then_inc(x_landed[c], 16)
            for c in range(CHUNKS):
                for t in range(TT):
                    group_to_hi(GROUP["x"] + TT * c + t, t, a_hi, 4 * c)
                split_hi(0, 2 * c, 0, first=True)
                split_hi(0, 2 * c + 1, 0, first=True)
            act.wait_ge(const_landed, 48)
            nc.scalar.activation(mask[:, :], mask_f[:, :], ACT.Copy).then_inc(mask_done, 1)
            act.wait_ge(angles_done, 1)
            nc.scalar.activation(cos_t[:, :, :], for_cos[:, :, :], ACT.Sin).then_inc(sines_done, 1)
            nc.scalar.activation(sin_t[:, :, :], for_sin[:, :, :], ACT.Sin).then_inc(sines_done, 1)

            def conv_store(j, half):
                act.wait_ge(conv_turned, j + 1)
                nc.scalar.activation(v_tok[:, :, bass.ds(j * T, T)], bank[:, 6 + half, :].rearrange("p (t n) -> p t n", t=TT),
                                     ACT.Copy).then_inc(conv_stored, 1)

            def conv_diagonals(j, taps, first=False):
                if not first:
                    act.wait_ge(taps_added, j)
                for k in range(2):
                    for m in range(taps):
                        nc.scalar.activation(diag[:, k, m, :], ident[:, :], ACT.Copy,
                                             scale=params[:, bass.ds(2 * j + k, 1), TAPS - taps + m]).then_inc(diag_done, 1)

            def conv_copy(j, half, first=False):
                act.wait_ge(conv_done, 2 * j + 2)
                if not first:
                    act.wait_ge(conv_turned, j)
                nc.scalar.activation(c_copy[:, :, :], bank[:, 4 + half, :].rearrange("p (k t) -> p k t", t=T),
                                     ACT.Copy).then_inc(conv_copied, 1)

            def conv_unit(j, q, half, first=False, store=True, taps=PE_TAPS):
                splits(q, 0, range(0, 4))
                if store:
                    conv_store(j - 2, half)
                splits(q, 0, range(4, 7))
                act.wait_ge(used, 8 * j + 8)
                if not first:
                    act.wait_ge(tile_free, TT * j)
                for k in range(2):
                    nc.scalar.activation(sig[:, k, :], pair(half)[:, k, T:2 * T], ACT.Sigmoid,
                                         bias=params[:, bass.ds(2 * j + k, 1), PARAMS - 1]).then_inc(sig_done, 1)
                splits(q, 0, range(7, 8))
                conv_diagonals(j, taps, first)

            act.wait_ge(params_done, 1)
            act.wait_ge(ident_landed, 16)
            conv_unit(0, 0, 0, first=True, store=False)
            conv_unit(1, 2, 1, store=False)
            conv_copy(0, 0, first=True)
            last = UNITS["conv"] - 1

            def conv_pair(i, taps=PE_TAPS):
                for k in range(2):
                    conv_unit(2 * i + k, 4 * i + 2 * k, k, taps=taps if k else PE_TAPS)
                    conv_copy(2 * i + k - 1, 1 - k)

            with act.Fori(1, last // 2) as i:
                conv_pair(i)
            conv_pair(last // 2, taps=LAST_PE_TAPS)
            conv_store(last - 1, 0)
            nc.scalar.activation(unused[:, :], eps[:, :], ACT.Sqrt)
            conv_copy(last, 1)
            conv_store(last, 1)
            for t in range(TT):
                deviations(0, t)
            nc.scalar.activation(unused[:, :], eps[:, :], ACT.Silu)
            for t in range(TT):
                norm_to_hi(0, t)

            def plain_units(stage, n):
                with act.Fori(0, n) as i:
                    splits(QUARTER[stage] + 2 * i, parity(stage), range(PIECES))

            def add_units(stage, k):
                plain_units(stage, UNITS[stage] - 1)
                last_unit(k, QUARTER[stage] + 2 * UNITS[stage] - 2, parity(stage))

            def sums_done(u, q, t):
                if t == 0:
                    act.wait_ge(first_done, u - UNIT["conv_out"] + 1)
                else:
                    act.wait_ge(used, 4 * q + 8)

            def project(layer, c):
                act.wait_ge(used, 4 * QUARTER[f"proj{layer}"] + c + 1)
                nc.scalar.activation(v_tok[:, :, chunk(c)], pair(c), ACT.Copy).then_inc(proj_stored, 1)

            def mlp(layer):
                stage = f"mlp{layer}"

                def slab(s, first=False, last=False):
                    for c in range(2 * CHUNKS):
                        q, u = QUARTER[stage] + 2 * c + 16 * s, UNIT[stage] + c + 8 * s
                        if 1 <= c <= CHUNKS:
                            for t in range(TT):
                                group_to_hi(GROUP[stage] + TT * (c - 1) + t, t, b_hi, 4 * (c - 1), off=ALL * s)

                        def rectify(t):
                            sums_done(u, q, t)
                            nc.scalar.activation(s_tok[:, t, :], pair(UNIT[stage] + c)[:, t, :], ACT.Relu).then_inc(relu_done, 1)

                        if c < CHUNKS:
                            rectify(0)
                        if last and c == 2 * CHUNKS - 1:
                            last_unit(NORMS.index(f"ln2_{layer}"), q, parity(stage), store=lambda n: project(layer, n))
                            return
                        splits(q, parity(stage), range(0, 7))
                        if first and c == 0:
                            for t in range(TT):
                                group_to_hi(GROUP[f"p{layer}"] + t, t, p_hi, 0, blocks=PLE // P)
                        if c < CHUNKS:
                            rectify(1)
                        splits(q, parity(stage), range(7, 8))
                        if first and c < CHUNKS:
                            nc.scalar.activation(x_tok[:, :, chunk(c)], x_tok[:, :, chunk(c)], ACT.Copy, scale=ALPHA).then_inc(scaled, 1)

                slab(0, first=True)
                with act.Fori(1, F // D - 1) as s:
                    slab(s)
                slab(F // D - 1, last=True)

            def ple(layer):
                gate = f"gate{layer}"
                for c in range(CHUNKS):
                    q, u = QUARTER[gate] + 2 * c, UNIT[gate] + c

                    def to_b(c):
                        for t in range(TT):
                            group_to_hi(GROUP[gate] + gate_group(t, c), t, b_hi, 4 * c)

                    def gate_tile(t):
                        sums_done(u, q, t)
                        n = TT * (CHUNKS * layer + c) + t
                        if c and layer == 0:
                            act.wait_ge(x_kept, n - 1)
                        if c and layer == 1:
                            act.wait_ge(stored[t], 16 * c)
                        nc.scalar.activation(s_tok[:, t, :], pair(u)[:, t, :], ACT.Sigmoid).then_inc(gate_done, 1)
                        act.wait_ge(x_new, n + 1)
                        if layer == 0:
                            nc.scalar.activation(x_tok[:, t, chunk(c)], s_tok[:, t, :], ACT.Copy).then_inc(x_kept, 1)
                        else:
                            act.dma_start(out_rows[:, t, chunk(c)], s_tok[:, t, :]).then_inc(stored[t], 16)

                    if c and layer == 0:
                        to_b(c - 1)
                    if layer == 0 and c == CHUNKS - 1:
                        last_unit(NORMS.index("kv_ln"), q, parity(gate), evacuate=gate_tile, extra=lambda: to_b(c), late=2)
                        return
                    more = range(PIECES) if c < CHUNKS - 1 else ()
                    gate_tile(0)
                    splits(q, parity(gate), more[0:7])
                    gate_tile(1)
                    splits(q, parity(gate), more[7:8])

            add_units("conv_out", NORMS.index("ln1_0"))
            mlp(0)
            ple(0)
            plain_units("kv", UNITS["kv"])

            def exps(h):
                act.wait_ge(soft_ready, h + 1)
                for t in range(TT):
                    s = soft[:, h % 2, seen(t):seen(t, G)]
                    nc.scalar.activation(s, s, ACT.Exp, bias=neg_max[:, h % 2, t:t + 1],
                                         accum_out=row_sum[:, h % 2, t:t + 1]).then_inc(exp_done, 1)

            def copy_probs(h):
                act.wait_ge(prob_turned, h + 1)
                nc.scalar.activation(prob_t(h % 2), turned_probs(h)[:, 0:sum(KEYS)], ACT.Copy).then_inc(prob_copied, 1)

            def store_o(h):
                act.wait_ge(o_done, h + 1)
                for t in range(TT):
                    nc.scalar.activation(o_tok[:, t, h * HD:(h + 1) * HD], output(h, t), ACT.Copy,
                                         scale=row_inv[:, h % 2, t:t + 1]).then_inc(o_stored, 1)

            for i in range(BLOCKS):
                for gap in range(G * PIECES):
                    h = HPU * (i - 1)
                    if i and gap in SCORES:
                        exps(h + SCORES[gap])
                    if i and gap in TURN_P:
                        copy_probs(h + TURN_P[gap])
                    if i and gap in PV:
                        store_o(h + PV[gap])
                    q = QUARTER["q"] + 2 * (G * i + gap // PIECES)
                    split_hi(q + 2, gap % PIECES, parity("q"))
            exps(LAST)
            for h in range(LAST, HEADS):
                if h + 1 < HEADS:
                    exps(h + 1)
                copy_probs(h)
                store_o(h)
            for t in range(TT):
                for c in range(CHUNKS):
                    group_to_hi(GROUP["o"] + CHUNKS * t + c, t, b_hi, 4 * c)
            add_units("attn_out", NORMS.index("ln1_1"))
            mlp(1)
            ple(1)

        @block.vector
        def _(dve):
            step = Count(dve, dve_step)
            link, mark = step.link, step.mark

            def split_lo(q, e, turned):
                slot = (e + turned) % PIECES
                dve.wait_ge(hi_done, 4 * q + e + 1)
                nc.vector.tensor_tensor(w_lo[:, slot, :, :], raw[:, e % RAW, :, :], w_hi[:, slot, :, :],
                                        ALU.subtract).then_inc(lo_done, 1)

            def splits(q, turned, pieces):
                for e in pieces:
                    split_lo(q + 2, e, turned)

            def group_to_lo(stage, n, t, hi, lo, kt, off=0, blocks=4):
                g = GROUP[stage] + n
                dve.wait_ge(group_hi, off + HIGH[stage] + n + 1)
                src = group_out(g)[:, 0:blocks, :] if stage != "conv_ln" else silu[:, g % 2, :, :]
                nc.vector.tensor_tensor(lo[:, kt:kt + blocks, tile(t)], src, hi[:, kt:kt + blocks, tile(t)],
                                        ALU.subtract).then_inc(group_free, 1)

            def variance(t, parts):
                step.wait(step.n)
                nc.vector.bn_aggr(mean_var[:, t, :], stats[:, t, 0:parts, :]).then_inc(var_done, 1)

            def norm(k, t, src, dst, with_lo=True):
                dve.wait_ge(std_done, TT * k + t + 1)
                link(nc.vector.reciprocal(rstd[:, t:t + 1], std[:, t:t + 1]))
                dve.wait_ge(gain_landed, 32 * (k + 1))

                def centre(c):
                    return mark(nc.vector.scalar_tensor_tensor(dst[:, t, chunk(c)], src[:, t, chunk(c)], mean_var[:, t, 0:1],
                                                               gain[:, chunk(c)], ALU.subtract, ALU.mult))

                centred = centre(0)
                for c in range(CHUNKS):
                    after = centre(c + 1) if c + 1 < CHUNKS else None
                    step.wait(centred)
                    nc.vector.scalar_tensor_tensor(dst[:, t, chunk(c)], dst[:, t, chunk(c)], rstd[:, t:t + 1],
                                                   shift[:, chunk(c)], ALU.mult, ALU.add).then_inc(rows_ready, 1)
                    centred = after
                    if with_lo and c:
                        norm_to_lo(k, t, c - 1)
                if with_lo:
                    norm_to_lo(k, t, CHUNKS - 1)

            def norm_to_lo(k, t, c):
                group_to_lo(NORMS[k], norm_group(NORMS[k], t, c), t, a_hi, a_lo, 4 * c)

            def last_unit(k, q, turned, evacuate, src, dst, extra=lambda: None, late=0, beside=None):
                evacuate(0)
                variance(0, CHUNKS)
                norm(k, 0, src, dst)
                def rest(pieces):
                    dve.wait_ge(lo_done, 4 * (q + 2) + RAW)
                    splits(q, turned, pieces)

                if late:
                    rest(range(RAW, RAW + late))
                evacuate(1)
                rest(range(RAW + late, PIECES))
                extra()
                variance(1, CHUNKS)
                norm(k, 1, src, dst, with_lo=beside is None)
                if beside is not None:
                    beside()
                    for c in range(CHUNKS):
                        norm_to_lo(k, 1, c)

            def sums_done(u, q, t):
                if t == 0:
                    dve.wait_ge(first_done, u - UNIT["conv_out"] + 1)
                else:
                    dve.wait_ge(used, 4 * q + 8)

            mark(nc.vector.memset(eps[:, :], EPS))
            mark(nc.vector.memset(u_pad[:, :, 0:PAD], 0.0))
            for c in range(CHUNKS):
                for t in range(TT):
                    group_to_lo("x", TT * c + t, t, a_hi, a_lo, 4 * c)
            dve.wait_ge(params_turned, 1)
            link(nc.vector.tensor_copy(params[:, :, 0:TAPS], bank[:, 4, 0:KT * TAPS].rearrange("p (c w) -> p c w", w=TAPS)))
            for n, r in ((TAPS, 2), (TAPS + 1, 0), (TAPS + 2, 1)):
                last = nc.vector.tensor_copy(params[:, :, n], bank[:, 5, r * KT:(r + 1) * KT])
            last.then_inc(params_done, 1)

            two_pi = 2 * np.pi
            part1 = 6.28125
            part2 = float(np.round((two_pi - part1) * 2.0 ** 20) / 2.0 ** 20)
            part3 = float(np.float32(two_pi - part1 - part2))
            magic = 1.5 * 2.0 ** 23
            pi = float(np.nextafter(np.float32(np.pi), np.float32(0)))
            dve.wait_ge(const_landed, 48)
            link(nc.vector.tensor_copy(pos_f[:, :], pos_i[:, :]))
            for t in range(TT):
                link(nc.vector.tensor_scalar(angle[:, t, :], inv_freq[:, :], pos_f[:, t:t + 1], None, ALU.mult))
            for dst, quarter in ((for_cos, 0.25), (for_sin, 0.0)):
                link(nc.vector.tensor_scalar(turns[:, :, :], angle[:, :, :], 1.0 / two_pi, quarter, ALU.mult, ALU.add))
                link(nc.vector.tensor_scalar(turns[:, :, :], turns[:, :, :], magic, magic, ALU.add, ALU.subtract))
                link(nc.vector.scalar_tensor_tensor(dst[:, :, :], turns[:, :, :], -part1, angle[:, :, :], ALU.mult, ALU.add))
                link(nc.vector.scalar_tensor_tensor(dst[:, :, :], turns[:, :, :], -part2, dst[:, :, :], ALU.mult, ALU.add))
                link(nc.vector.scalar_tensor_tensor(dst[:, :, :], turns[:, :, :], -part3, dst[:, :, :], ALU.mult, ALU.add))
                link(nc.vector.tensor_scalar(dst[:, :, :], dst[:, :, :], quarter * two_pi, pi, ALU.add, ALU.min))
                n = nc.vector.tensor_scalar(dst[:, :, :], dst[:, :, :], -pi, None, ALU.max)
                if quarter:
                    link(n)
            n.then_inc(angles_done, 1)
            dve.wait_ge(sines_done, 2)
            link(nc.vector.tensor_scalar(nsin_t[:, :, :], sin_t[:, :, :], -1.0, None, ALU.mult))

            def conv_stats(j):
                dve.wait_ge(conv_stored, j + 1)
                for t in range(TT):
                    mark(nc.vector.bn_stats(stats[:, t, bass.ds(j, 1), :], v_tok[:, t, bass.ds(j * T, T)]))

            def conv_unit(j, half, first=False, second=False, mine=TAPS - PE_TAPS):
                if not first:
                    dve.wait_ge(conv_done, 2 * j)
                    dve.wait_ge(taps_added, j)
                link(nc.vector.tensor_copy(taps[:, :, :], params[:, bass.ds(2 * j, 2), :]))
                for k in range(2):
                    dve.wait_ge(sig_done, 2 * j + k + 1)
                    n = nc.vector.scalar_tensor_tensor(u_pad[:, k, PAD:PAD + T], pair(half)[:, k, 0:T],
                                                       taps[:, k, TAPS + 1:TAPS + 2], sig[:, k, :], ALU.add, ALU.mult)
                    n.then_inc(tile_free, 1)
                dve.wait_ge(tile_free, TT * j + 2)
                if not (first or second):
                    dve.wait_ge(conv_copied, j - 1)
                marks = [None, None]
                for w in range(mine):
                    for k in range(2):
                        acc = bank[:, 4 + half, k * T:(k + 1) * T]
                        u = u_pad[:, k, w:w + T]
                        if w == 0:
                            n = nc.vector.tensor_scalar(acc, u, taps[:, k, 0:1], taps[:, k, TAPS:TAPS + 1], ALU.mult, ALU.add)
                        else:
                            step.wait(marks[k])
                            n = nc.vector.scalar_tensor_tensor(acc, u, taps[:, k, w:w + 1], acc, ALU.mult, ALU.add)
                        if w < mine - 1:
                            marks[k] = mark(n)
                        else:
                            n.then_inc(conv_done, 1)

            conv_unit(0, 0, first=True)
            conv_unit(1, 1, second=True)

            def conv_pair(i, mine=TAPS - PE_TAPS):
                for k in range(2):
                    conv_stats(2 * i + k)
                    conv_unit(2 * i + 2 + k, k, mine=mine if k else TAPS - PE_TAPS)

            rounds = UNITS["conv"] // 2 - 2
            with dve.Fori(0, rounds) as i:
                step.enter(i, 2 * (TT + 1 + 2 * (TAPS - PE_TAPS - 1)))
                conv_pair(i)
                step.leave(rounds)
            conv_pair(rounds, mine=TAPS - LAST_PE_TAPS)
            conv_stats(UNITS["conv"] - 2)
            conv_stats(UNITS["conv"] - 1)
            for t in range(TT):
                variance(t, UNITS["conv"])
            for t in range(TT):
                norm(0, t, v_tok, v_tok)

            def add_units(stage, k):
                for c in range(CHUNKS):
                    u, q = UNIT[stage] + c, QUARTER[stage] + 2 * c

                    def add(t):
                        sums_done(u, q, t)
                        x = x_tok[:, t, chunk(c)]
                        nc.vector.scalar_tensor_tensor(x, x, ALPHA, pair(u)[:, t, :], ALU.mult, ALU.add).then_inc(tile_free, 1)
                        dve.wait_ge(tile_free, taken(u, t))
                        mark(nc.vector.bn_stats(stats[:, t, c, :], x))

                    if c == CHUNKS - 1:
                        last_unit(k, q, parity(stage), add, x_tok, x_tok)
                    else:
                        add(0)
                        splits(q, parity(stage), range(0, 7))
                        add(1)
                        splits(q, parity(stage), range(7, 8))

            def project(layer):
                proj = f"proj{layer}"
                for e in range(4):
                    split_lo(QUARTER[proj] + 2, e, parity(proj))

            def mlp(layer):
                stage = f"mlp{layer}"
                def slab(s, first=False, last=False):
                    for c in range(2 * CHUNKS):
                        q = QUARTER[stage] + 2 * c + 16 * s
                        u = UNIT[stage] + c + 8 * s
                        ps = pair(UNIT[stage] + c)

                        def up(t):
                            dve.wait_ge(relu_done, TT * (CHUNKS * (4 * layer + s) + c) + t + 1)
                            nc.vector.tensor_tensor(s_tok[:, t, :], s_tok[:, t, :], ps[:, t, :], ALU.mult).then_inc(tile_free, 1)

                        def down(t):
                            sums_done(u, q, t)
                            x = x_tok[:, t, chunk(c - CHUNKS)]
                            nc.vector.tensor_tensor(x, x, ps[:, t, :], ALU.add).then_inc(tile_free, 1)
                            if last:
                                dve.wait_ge(tile_free, taken(u, t))
                                mark(nc.vector.bn_stats(stats[:, t, c - CHUNKS, :], x))

                        if 1 <= c <= CHUNKS:
                            for t in range(TT):
                                group_to_lo(stage, TT * (c - 1) + t, t, b_hi, b_lo, 4 * (c - 1), off=ALL * s)
                        if last and c == 2 * CHUNKS - 1:
                            last_unit(NORMS.index(f"ln2_{layer}"), q, parity(stage), down, x_tok, x_tok, beside=lambda: project(layer))
                            return
                        if first and c == CHUNKS:
                            dve.wait_ge(scaled, CHUNKS * (layer + 1))
                        evacuate = up if c < CHUNKS else down
                        evacuate(0)
                        splits(q, parity(stage), range(0, 7))
                        if first and c == 0:
                            for t in range(TT):
                                group_to_lo(f"p{layer}", t, t, p_hi, p_lo, 0, blocks=PLE // P)
                        evacuate(1)
                        splits(q, parity(stage), range(7, 8))

                slab(0, first=True)
                with dve.Fori(1, F // D - 1) as s:
                    slab(s)
                slab(F // D - 1, last=True)

            def ple(layer):
                proj, gate = f"proj{layer}", f"gate{layer}"
                for c in range(CHUNKS):
                    q, u = QUARTER[gate] + 2 * c, UNIT[gate] + c

                    def to_b(c):
                        for t in range(TT):
                            group_to_lo(gate, gate_group(t, c), t, b_hi, b_lo, 4 * c)

                    def gate_tile(t):
                        dve.wait_ge(proj_stored, CHUNKS * layer + c + 1)
                        dve.wait_ge(gate_done, TT * (CHUNKS * layer + c) + t + 1)
                        nc.vector.tensor_tensor(s_tok[:, t, :], s_tok[:, t, :], v_tok[:, t, chunk(c)], ALU.mult).then_inc(tile_free, 1)
                        dve.wait_ge(tile_free, taken(u, t))
                        n = nc.vector.tensor_tensor(s_tok[:, t, :], s_tok[:, t, :], x_tok[:, t, chunk(c)], ALU.add)
                        if layer == 0:
                            link(n)
                            n = nc.vector.bn_stats(stats[:, t, c, :], s_tok[:, t, :])
                        n.then_inc(x_new, 1)
                        if layer == 0 and c == CHUNKS - 1:
                            dve.wait_ge(x_kept, TT * c + t + 1)

                    if c and layer == 0:
                        to_b(c - 1)
                    if layer == 0 and c == CHUNKS - 1:
                        last_unit(NORMS.index("kv_ln"), q, parity(gate), gate_tile, x_tok, v_tok, extra=lambda: to_b(c), late=2)
                        return
                    more = range(PIECES) if c < CHUNKS - 1 else ()
                    gate_tile(0)
                    splits(q, parity(gate), more[0:7])
                    gate_tile(1)
                    splits(q, parity(gate), more[7:8])

            def rotate(ps, dst, t):
                def halves(x):
                    return x.rearrange("p (h s f) -> p h s f", s=2, f=HALF)

                def table(x, n):
                    return x[:, t:t + 1, :].broadcast_to([P, n, HALF])

                mark(nc.vector.tensor_tensor(dst.rearrange("p (h f) -> p h f", f=HALF), ps.rearrange("p (h f) -> p h f", f=HALF),
                                             table(cos_t, 2 * HPU), ALU.mult))
                mark(nc.vector.tensor_tensor(halves(rot_tmp[:, :])[:, :, 0, :], halves(ps)[:, :, 1, :], table(nsin_t, HPU), ALU.mult))
                link(nc.vector.tensor_tensor(halves(rot_tmp[:, :])[:, :, 1, :], halves(ps)[:, :, 0, :], table(sin_t, HPU), ALU.mult))
                return nc.vector.tensor_tensor(dst, dst, rot_tmp[:, :], ALU.add)

            def keys_and_values():
                for c in range(2 * CHUNKS):
                    q, u = QUARTER["kv"] + 2 * c, UNIT["kv"] + c
                    if 1 <= c <= CHUNKS:
                        for t in range(TT):
                            n = TT * (c - 1) + t
                            dve.wait_ge(group_done, GROUP["k"] + n + 1)
                            nc.vector.tensor_copy(k_t[:, HPU * (c - 1):HPU * c, tile(t)], group_out(GROUP["k"] + n)).then_inc(group_free, 1)

                    def evacuate(t):
                        sums_done(u, q, t)
                        if c < CHUNKS:
                            rotate(pair(u)[:, t, :], s_tok[:, t, :], t).then_inc(tile_free, 1)
                            dve.wait_ge(tile_free, taken(u, t))
                        else:
                            nc.vector.tensor_copy(v_tok[:, t, chunk(c - CHUNKS)], pair(u)[:, t, :]).then_inc(tile_free, 1)

                    evacuate(0)
                    splits(q, parity("kv"), range(0, 7))
                    evacuate(1)
                    splits(q, parity("kv"), range(7, 8))

            dve.wait_ge(lo_done, 4 * QUARTER["conv_out"] + PIECES)
            add_units("conv_out", NORMS.index("ln1_0"))
            mlp(0)
            ple(0)
            keys_and_values()

            def masked_max(h):
                dve.wait_ge(scores_done, h + 1)
                if h >= 2:
                    dve.wait_ge(o_done, h - 1)
                for t in range(TT):
                    mark(nc.vector.tensor_tensor_reduce(out=soft[:, h % 2, seen(t):seen(t, G)], in0=all_scores(h, t),
                                                        in1=mask[:, seen(t):seen(t, G)], scale=SCALE, scalar=MASKED,
                                                        op0=ALU.add, op1=ALU.max, accum_out=row_max[:, h % 2, t:t + 1]))
                step.wait(step.n)
                nc.vector.tensor_scalar(neg_max[:, h % 2, :], row_max[:, h % 2, :], -1.0, None, ALU.mult).then_inc(soft_ready, 1)

            def add_groups(h):
                dve.wait_ge(exp_done, 2 * h + 2)
                mark(nc.vector.reciprocal(row_inv[:, h % 2, :], row_sum[:, h % 2, :]))
                part = [[soft[:, h % 2, seen(t, g):seen(t, g + 1)] for g in range(G)] for t in range(TT)]
                marks = [mark(nc.vector.tensor_tensor(part[t][0], part[t][0], part[t][1], ALU.add)) for t in range(TT)]
                for t in range(TT):
                    step.wait(marks[t])
                    n = nc.vector.tensor_tensor(part[t][0], part[t][0], part[t][2], ALU.add)
                n.then_inc(prob_done, 1)

            def copy_q(i, g, t):
                dve.wait_ge(q_turned, TT * (G * i + g) + t + 1)
                nc.vector.tensor_copy(q_t[:, g, :, t * P:(t + 1) * P],
                                      bank[:, TURN, :].rearrange("p (h t) -> p h t", t=P)).then_inc(q_copied, 1)

            def rotate_q(i, g, t):
                u = G * i + g
                dve.wait_ge(used, 4 * (QUARTER["q"] + 2 * u) + 8)
                if u:
                    dve.wait_ge(q_turned, TT * (u - 1) + t + 1)
                rotate(pair(UNIT["q"] + u)[:, t, :], q_rot[:, t, :], t).then_inc(tile_free, 1)
                dve.wait_ge(tile_free, taken(UNIT["q"] + u, t))

            for i in range(BLOCKS):
                for gap in range(G * PIECES):
                    h = HPU * (i - 1)
                    if gap in TURN_Q and (i or gap > 3):
                        copy_q(i - (gap <= 3), *TURN_Q[gap])
                    if gap in ROTATE and (i or gap > 3):
                        rotate_q(i - (gap <= 3), *ROTATE[gap])
                    if i and gap in SCORES:
                        masked_max(h + SCORES[gap])
                        add_groups(h + SCORES[gap])
                    q = QUARTER["q"] + 2 * (G * i + gap // PIECES)
                    split_lo(q + 2, gap % PIECES, parity("q"))
            for t in range(TT):
                rotate_q(BLOCKS - 1, G - 1, t)
            for t in range(TT):
                copy_q(BLOCKS - 1, G - 1, t)
            masked_max(LAST)
            masked_max(LAST + 1)
            for h in range(LAST, HEADS):
                add_groups(h)
                if h + 2 < HEADS:
                    masked_max(h + 2)
            for t in range(TT):
                for c in range(CHUNKS):
                    group_to_lo("o", CHUNKS * t + c, t, b_hi, b_lo, 4 * c)
            add_units("attn_out", NORMS.index("ln1_1"))
            mlp(1)
            ple(1)

        @block.tensor
        def _(pe):
            def products(slot, hi, lo, kt, t, ps, first, last):
                for k in range(KP):
                    x_hi, x_lo = (x[:, kt + k, tile(t)] for x in (hi, lo))
                    for n, (x, w) in enumerate(((x_hi, w_hi), (x_hi, w_lo), (x_lo, w_hi))):
                        ins = nc.tensor.matmul(ps[:, t, :], x, w[:, slot, k, :], start=first and k == 0 and n == 0,
                                               stop=last and k == KP - 1 and n == 2)
                return ins

            def unit(q, u, turned, x, ps, ready=None, between=None, tiles_apart=True):
                order = [(t, e) for t in range(TT) for e in range(PIECES)]
                if not tiles_apart:
                    order.sort(key=lambda te: te[1])
                for t, e in order:
                    if between is not None:
                        between(t, e)
                    if e == 0:
                        pe.wait_ge(tile_free, taken(u - 2, t))
                    if ready is not None and e % 2 == 0:
                        ready(t, e // 2)
                    if t == 0:
                        pe.wait_ge(lo_done, 4 * q + e + 1)
                    ins = products((e + turned) % PIECES, *x, KP * e, t, ps, e == 0, e == PIECES - 1)
                    if t == TT - 1:
                        ins.then_inc(used, 1)
                    elif e == PIECES - 1:
                        ins.then_inc(first_done, 1)

            def split_wait(stage, major="t", off=0):
                def ready(t, c):
                    n = norm_group(stage, t, c) if major == "t" else TT * c + t
                    pe.wait_ge(group_free, GROUP[stage] + n + 1 + off)
                return ready

            def turn_group(g, src, t, off=0, cols=0, blocks=4):
                if g >= 4:
                    pe.wait_ge(group_free, g - 3 + off)
                for k in range(blocks):
                    n = nc.tensor.transpose(group_out(g)[:, k, :], src[:, t, cols + k * P:cols + (k + 1) * P], ident[:, :])
                n.then_inc(group_done, 1)

            def turn_norm(name, t, c, src):
                pe.wait_ge(rows_ready, ROWS[name] + CHUNKS * t + c + 1)
                turn_group(GROUP[name] + norm_group(name, t, c), src, t, cols=c * COLS)

            def turn_at(places, name, half, src):
                def between(t, e):
                    for c in range(CHUNKS):
                        if places[c] == (t, e):
                            turn_norm(name, half, c, src)
                return between

            pe.wait_ge(ident_landed, 16)
            for c in range(CHUNKS):
                pe.wait_ge(x_landed[c], 16)
                for t in range(TT):
                    turn_group(GROUP["x"] + TT * c + t, x_tok, t, cols=c * COLS)

            def turn_params():
                pe.wait_ge(rows_landed, 48)
                pe.wait_ge(group_free, GROUP["x"] + ALL)
                for c in range(KT):
                    nc.tensor.transpose(bank[:, 4, c * TAPS:(c + 1) * TAPS], dw_rows[:, c * P:(c + 1) * P], ident[0:TAPS, 0:TAPS])
                nc.tensor.transpose(bank[:, 5, 0:3 * KT], bias_rows[:, :], ident[0:3 * KT, 0:3 * KT]).then_inc(params_turned, 1)

            def conv_taps(j, half, taps=PE_TAPS, early=False):
                pe.wait_ge(tile_free, TT * j + 2)
                if not early:
                    pe.wait_ge(conv_stored, j - 1)
                for k in range(2):
                    for m in range(taps):
                        pe.wait_ge(diag_done, 2 * PE_TAPS * j + taps * k + m + 1)
                        for t in range(TT):
                            w = TAPS - taps + m + t * P
                            n = nc.tensor.matmul(bank[:, 6 + half, t * T + k * P:t * T + (k + 1) * P], u_pad[:, k, w:w + P], diag[:, k, m, :],
                                                 start=k == 0 and m == 0 and t == 0, stop=False, skip_group_check=True)
                n.then_inc(taps_added, 1)

            def conv_turn(j, half):
                pe.wait_ge(conv_copied, j + 1)
                for t in range(TT):
                    for k in range(2):
                        n = nc.tensor.matmul(bank[:, 6 + half, t * T + k * P:t * T + (k + 1) * P], c_copy[:, k, t * P:(t + 1) * P], ident[:, :],
                                             start=False, stop=True, skip_group_check=True)
                n.then_inc(conv_turned, 1)

            def conv_unit(j, q, half, turn=None, taps=None, first=False):
                if not first:
                    pe.wait_ge(tile_free, taken(j - 2, 1))
                for e in range(PIECES):
                    if e == 2 and turn is not None:
                        turn()
                    if e == 4 and taps is not None:
                        taps()
                    if e % 2 == 0:
                        split_wait("x", major="c")(1, e // 2)
                    pe.wait_ge(lo_done, 4 * q + e + 1)
                    side = e % 2
                    for k in range(2 * KP):
                        kt = 2 * KP * (e // 2) + k
                        for b in range(2):
                            cols = slice(k % 2 * T + b * P, k % 2 * T + (b + 1) * P)
                            ws = [w[:, e, k // 2, cols] for w in (w_hi, w_lo)]
                            xs = [x[:, kt, :] for x in (a_hi, a_lo)]
                            for n, (w, x) in enumerate(((ws[0], xs[0]), (ws[1], xs[0]), (ws[0], xs[1]))):
                                ins = nc.tensor.matmul(pair(half)[:, b, side * T:(side + 1) * T], w, x,
                                                       start=kt == 0 and side == 0 and n == 0,
                                                       stop=kt == KT - 1 and n == 2, skip_group_check=True)
                    ins.then_inc(used, 1)

            conv_unit(0, 0, 0, turn=turn_params, first=True)
            conv_unit(1, 2, 1, taps=lambda: conv_taps(0, 0, early=True), first=True)
            conv_unit(2, 4, 0, turn=lambda: conv_turn(0, 0), taps=lambda: conv_taps(1, 1, early=True))
            conv_unit(3, 6, 1, turn=lambda: conv_turn(1, 1), taps=lambda: conv_taps(2, 0))
            with pe.Fori(2, UNITS["conv"] // 2) as i:
                for k in range(2):
                    j = 2 * i + k
                    conv_unit(j, 2 * j, k, turn=lambda: conv_turn(j - 2, k), taps=lambda: conv_taps(j - 1, 1 - k))
            last = UNITS["conv"] - 1
            conv_taps(last, 1, taps=LAST_PE_TAPS)
            conv_turn(last - 1, 0)
            conv_turn(last, 1)

            def add_units(stage, x, ready, between, name):
                def one(c, u, q, **more):
                    unit(q, u, parity(stage), x, pair(UNIT[stage] + c), **more)

                one(0, UNIT[stage], QUARTER[stage], ready=ready, between=between)
                one(1, UNIT[stage] + 1, QUARTER[stage] + 2)
                one(2, UNIT[stage] + 2, QUARTER[stage] + 4)
                one(3, UNIT[stage] + 3, QUARTER[stage] + 6, between=turn_at(FIRST, name, 0, x_tok))

            def mlp(layer):
                stage, name = f"mlp{layer}", f"ln1_{layer}"

                def turn_p(t, e):
                    turn_at(SOON, name, 1, x_tok)(t, e)
                    if (t, e) == (1, 6):
                        pe.wait_ge(p_landed, 16 * (layer + 1))
                        for n in range(TT):
                            turn_group(GROUP[f"p{layer}"] + n, p_tok, n, blocks=PLE // P)

                def slab(s, first=False, last=False):
                    for c in range(2 * CHUNKS):
                        q, u = QUARTER[stage] + 2 * c + 16 * s, UNIT[stage] + c + 8 * s

                        def between(t, e):
                            if first and c == 0:
                                turn_p(t, e)
                            if last and c == 2 * CHUNKS - 1:
                                turn_at(FIRST, f"ln2_{layer}", 0, x_tok)(t, e)
                            if (t, e) == (0, 6 if first and c == 1 else 2) and 1 <= c <= CHUNKS:
                                for n in range(TT):
                                    pe.wait_ge(tile_free, taken(u - 1, n))
                                    turn_group(GROUP[stage] + TT * (c - 1) + n, s_tok, n, off=ALL * s)

                        ready = None
                        if first and c == 0:
                            ready = split_wait(name)
                        if c == CHUNKS:
                            ready = split_wait(stage, major="c", off=ALL * s)
                        x = (a_hi, a_lo) if c < CHUNKS else (b_hi, b_lo)
                        unit(q, u, parity(stage), x, pair(UNIT[stage] + c), ready=ready, between=between)

                slab(0, first=True)
                with pe.Fori(1, F // D - 1) as s:
                    slab(s)
                slab(F // D - 1, last=True)

            def ple(layer):
                proj, gate, name = f"proj{layer}", f"gate{layer}", f"ln2_{layer}"
                pe.wait_ge(group_free, GROUP[f"p{layer}"] + TT)
                for c in range(CHUNKS):
                    if c < 2:
                        pe.wait_ge(tile_free, taken(UNIT[gate] - 2 + c, 1))
                    else:
                        pe.wait_ge(proj_stored, CHUNKS * layer + c - 1)
                    pe.wait_ge(lo_done, 4 * QUARTER[proj] + c + 1)
                    for t in range(TT):
                        ins = products((c + parity(proj)) % PIECES, p_hi, p_lo, 0, t, pair(c), True, True)
                    ins.then_inc(used, 1)
                for c in range(CHUNKS):
                    def between(t, e):
                        if (t, e) == (0, 0) and c < 2:
                            pe.wait_ge(proj_stored, CHUNKS * layer + 3 + c)
                        if c == 0:
                            turn_at(LATER, name, 1, x_tok)(t, e)
                        if (t, e) == (0, 6) and c and layer == 0:
                            turn_gate(c - 1)
                        if c == CHUNKS - 1 and layer == 0:
                            turn_at(FIRST, "kv_ln", 0, v_tok)(t, e)
                    unit(QUARTER[gate] + 2 * c, UNIT[gate] + c, parity(gate), (a_hi, a_lo), pair(UNIT[gate] + c),
                         ready=split_wait(name) if c == 0 else None, between=between)
            def turn_gate(c):
                for t in range(TT):
                    pe.wait_ge(x_new, TT * c + t + 1)
                    turn_group(GROUP["gate0"] + gate_group(t, c), s_tok, t)

            for c in range(CHUNKS):
                turn_norm("conv_ln", 0, c, v_tok)
            add_units("conv_out", (a_hi, a_lo), split_wait("conv_ln"), turn_at(EAGER, "conv_ln", 1, v_tok), "ln1_0")
            mlp(0)
            ple(0)

            def kv_between(c):
                def between(t, e):
                    if c == 0:
                        if (t, e) == (0, 6):
                            turn_gate(CHUNKS - 1)
                        turn_at(SOON, "kv_ln", 1, v_tok)(t, e)
                    if (t, e) == (0, 7) and 1 <= c <= CHUNKS:
                        for n in range(TT):
                            pe.wait_ge(tile_free, taken(UNIT["kv"] + c - 1, n))
                            turn_group(GROUP["k"] + TT * (c - 1) + n, s_tok, n)
                return between

            for c in range(2 * CHUNKS):
                unit(QUARTER["kv"] + 2 * c, UNIT["kv"] + c, parity("kv"), (a_hi, a_lo), pair(UNIT["kv"] + c),
                     ready=split_wait("kv_ln") if c == 0 else None, between=kv_between(c))

            def before(h):
                return h if h <= LAST else h - 1

            def scores(h):
                hh = h % HPU
                if h % HPU == 0:
                    pe.wait_ge(q_copied, TT * G * (h // HPU + 1))
                if h:
                    pe.wait_ge(soft_ready, before(h))
                    pe.wait_ge(o_stored, TT * before(h))
                for g in range(G):
                    nc.tensor.matmul(scores_0(h, g), q_t[:, g, hh, 0:P], k_t[:, h, 0:P], start=True, stop=True)
                for g in range(G):
                    n = nc.tensor.matmul(scores_1(h, g), q_t[:, g, hh, P:T], k_t[:, h, :], start=True, stop=True)
                n.then_inc(scores_done, 1)

            def turn_probs(h, copied):
                pe.wait_ge(prob_done, h + 1)
                if copied:
                    pe.wait_ge(q_copied, copied)
                if h:
                    pe.wait_ge(prob_copied, before(h))
                dst = turned_probs(h)
                part = [soft[:, h % 2, seen(t):seen(t, 1)] for t in range(TT)]
                nc.tensor.transpose(dst[:, 0:P], part[0], ident[:, :])
                nc.tensor.transpose(dst[:, P:2 * P], part[1][:, 0:P], ident[:, :])
                nc.tensor.transpose(dst[:, 2 * P:3 * P], part[1][:, P:T], ident[:, :]).then_inc(prob_turned, 1)

            def outputs(h):
                pe.wait_ge(prob_copied, h + 1)
                p_t = prob_t(h % 2)
                cols = slice(h * HD, (h + 1) * HD)
                nc.tensor.matmul(output(h, 0), p_t[:, 0:P], v_tok[:, 0, cols], start=True, stop=True)
                nc.tensor.matmul(output(h, 1), p_t[:, P:2 * P], v_tok[:, 0, cols], start=True, stop=False)
                nc.tensor.matmul(output(h, 1), p_t[:, 2 * P:3 * P], v_tok[:, 1, cols], start=False, stop=True).then_inc(o_done, 1)

            turned = [0]

            def turn_q(i, g, t, probs):
                pe.wait_ge(tile_free, taken(UNIT["q"] + G * i + g, t))
                if turned[0]:
                    pe.wait_ge(q_copied, turned[0])
                if probs:
                    pe.wait_ge(prob_copied, probs)
                for hh in range(HPU):
                    n = nc.tensor.transpose(bank[:, TURN, hh * P:(hh + 1) * P], q_rot[:, t, hh * HD:(hh + 1) * HD], ident[:, :])
                n.then_inc(q_turned, 1)
                turned[0] += 1

            def q_between(i, g):
                def between(t, e):
                    if t:
                        return
                    gap, h = g * PIECES + e, HPU * (i - 1)
                    if gap in TURN_Q and (i or gap > 3):
                        probs = h + sum(x < gap for x in TURN_P) if i else 0
                        turn_q(i - (gap <= 3), *TURN_Q[gap], probs)
                    if i and gap in SCORES:
                        scores(h + SCORES[gap])
                    if i and gap in TURN_P:
                        turn_probs(h + TURN_P[gap], turned[0])
                    if i and gap in PV:
                        outputs(h + PV[gap])
                return between

            for i in range(BLOCKS):
                for g in range(G):
                    u = G * i + g
                    unit(QUARTER["q"] + 2 * u, UNIT["q"] + u, parity("q"), (b_hi, b_lo), pair(UNIT["q"] + u),
                         between=q_between(i, g), tiles_apart=False)
            turn_q(BLOCKS - 1, G - 1, 0, LAST)
            turn_q(BLOCKS - 1, G - 1, 1, LAST)
            scores(LAST)
            for h in range(LAST, HEADS):
                if h + 1 < HEADS:
                    scores(h + 1)
                turn_probs(h, turned[0])
                outputs(h)
            pe.wait_ge(o_stored, TT * HEADS)
            for t in range(TT):
                for c in range(CHUNKS):
                    turn_group(GROUP["o"] + CHUNKS * t + c, o_tok, t, cols=c * COLS)
            add_units("attn_out", (b_hi, b_lo), split_wait("o"), None, "ln1_1")
            mlp(1)
            ple(1)


_INS = ("x", "p", "positions", "conv_w_in", "conv_b_in", "conv_dw", "conv_dw_b", "conv_ln_g", "conv_ln_b",
        "conv_w_out", "kv_ln_g", "kv_ln_b", "w_kv", "attn_w_q", "attn_w_o", "ln1_g", "ln1_b", "mlp_up",
        "mlp_down", "ln2_g", "ln2_b", "ple_proj", "ple_gate")


def shape_constants():
    freq = 10000.0 ** (-np.arange(HALF, dtype=np.float32) * np.float32(2.0 / HD))
    parts = [np.eye(P), np.broadcast_to(freq, (P, HALF))]
    for t, keys in enumerate(KEYS):
        back = (t * P + np.arange(P))[:, None] - np.arange(keys)[None, :]
        for window, dilation in WINDOWS:
            inside = (back >= 0) & (back <= window) & (back % dilation == 0)
            parts.append(np.where(inside, 0.0, MASKED))
    return np.ascontiguousarray(np.concatenate(parts, axis=1).astype(np.float32))


def kernel(**inputs):
    import concourse.bacc as bacc
    from concourse.bass_utils import run_bass_kernel_spmd

    nc = bacc.Bacc("TRN2", target_bir_lowering=False, num_devices=1)
    arrays, args = {}, {}
    for name in _INS + ("consts",):
        a = shape_constants() if name == "consts" else np.ascontiguousarray(inputs[name])
        arrays[f"in_{name}"] = a
        args[name] = nc.dram_tensor(f"in_{name}", a.shape, mybir.dt.from_np(a.dtype), kind="ExternalInput").ap()
    out = nc.dram_tensor("out", (1, T, D), F32, kind="ExternalOutput").ap()
    trunk(nc, args, out)
    result = run_bass_kernel_spmd(nc, [arrays], core_ids=[0])
    return result.results[0]["out"]
```
